# Optimizing a Trainium2 kernel written in Bass

```python
import jax
import jax.numpy as jnp
from jax import lax
import numpy as np

D_MODEL = 1024
BATCH = 1
SEQ = 256
DEPTH = 2

MEM_LEN = 256
CONV_WIDTH = 512
CONV_K = 3
SG_WIDTH = 512
SG_GROUPS = 4
SG_GROUP_DIM = SG_WIDTH // SG_GROUPS
CHUNK = 128
FOX_HEADS = 8
FOX_HEAD_DIM = 64
FOX_WIDTH = FOX_HEADS * FOX_HEAD_DIM
Q_BLOCK = 128
FORGET_BIAS_CENTER = 3.0
N_BRANCH = 3
BRANCH_WIDTH = 512
XA_HEADS = 4
XA_HEAD_DIM = D_MODEL // XA_HEADS
D_FF = 2816
RMS_EPS = 1e-6
SPLIT_SIZES = (CONV_WIDTH, CONV_WIDTH, CONV_WIDTH, SG_WIDTH, SG_WIDTH,
               FOX_WIDTH, FOX_WIDTH, FOX_WIDTH, FOX_HEADS, N_BRANCH * D_MODEL)
D_IN_PROJ = sum(SPLIT_SIZES)

kernel_name = "hybrid_conv_gmlp_fox_macaron"

def rmsnorm(x, g):
    xf = x.astype(jnp.float32)
    y = xf * lax.rsqrt(jnp.mean(xf * xf, axis=-1, keepdims=True) + RMS_EPS)
    return (y * g.astype(jnp.float32)).astype(x.dtype)

def swiglu(h, w_gate, w_up, w_down):
    return (jax.nn.silu(h @ w_gate) * (h @ w_up)) @ w_down

def short_conv_mixer(b_gate, c_gate, h, conv_w):
    z = c_gate * h
    s = z.shape[1]
    zp = jnp.pad(z, ((0, 0), (CONV_K - 1, 0), (0, 0)))
    y = sum(conv_w[k] * zp[:, k:k + s] for k in range(CONV_K))
    return b_gate * y

def spatial_gating_mixer(u, v, v_norm_g, w_s, b_s):
    bsz, s, _ = v.shape
    u = jax.nn.gelu(u)
    v = rmsnorm(jax.nn.gelu(v), v_norm_g)
    vc = v.reshape(bsz, s // CHUNK, CHUNK, SG_GROUPS, SG_GROUP_DIM)
    causal = jnp.tril(jnp.ones((CHUNK, CHUNK), dtype=bool))
    w = jnp.where(causal[None], w_s, 0.0).astype(v.dtype)
    sv = jnp.einsum('gts,bnsgc->bntgc', w, vc) + b_s.T[:, :, None].astype(v.dtype)
    return u * sv.reshape(bsz, s, SG_WIDTH)

def forgetting_attention(q, k, v, f_logit, b_f):
    bsz, s, _ = q.shape
    q = q.reshape(bsz, s, FOX_HEADS, FOX_HEAD_DIM)
    k = k.reshape(bsz, s, FOX_HEADS, FOX_HEAD_DIM)
    v = v.reshape(bsz, s, FOX_HEADS, FOX_HEAD_DIM)
    log_f = jax.nn.log_sigmoid(f_logit.astype(jnp.float32) + b_f.astype(jnp.float32))
    c = jnp.cumsum(log_f, axis=1).transpose(0, 2, 1)
    scale = FOX_HEAD_DIM ** -0.5
    kpos = jnp.arange(s)

    def block(i):
        start = i * Q_BLOCK
        qb = lax.dynamic_slice_in_dim(q, start, Q_BLOCK, axis=1)
        cq = lax.dynamic_slice_in_dim(c, start, Q_BLOCK, axis=2)
        logits = jnp.einsum('bqhd,bkhd->bhqk', qb, k,
                            preferred_element_type=jnp.float32) * scale
        logits = logits + cq[..., :, None] - c[..., None, :]
        qpos = start + jnp.arange(Q_BLOCK)
        logits = jnp.where(kpos[None, :] <= qpos[:, None], logits, -jnp.inf)
        p = jax.nn.softmax(logits, axis=-1)
        return jnp.einsum('bhqk,bkhd->bqhd', p.astype(v.dtype), v)

    out = lax.map(block, jnp.arange(s // Q_BLOCK))
    return out.transpose(1, 0, 2, 3, 4).reshape(bsz, s, FOX_WIDTH)

def memory_cross_attention(h, m, wq, wk, wv, wo):
    bsz, s, _ = h.shape
    q = (h @ wq).reshape(bsz, s, XA_HEADS, XA_HEAD_DIM)
    k = (m @ wk).reshape(bsz, m.shape[1], XA_HEADS, XA_HEAD_DIM)
    v = (m @ wv).reshape(bsz, m.shape[1], XA_HEADS, XA_HEAD_DIM)
    logits = jnp.einsum('bqhd,bkhd->bhqk', q, k,
                        preferred_element_type=jnp.float32) * (XA_HEAD_DIM ** -0.5)
    p = jax.nn.softmax(logits, axis=-1)
    o = jnp.einsum('bhqk,bkhd->bqhd', p.astype(v.dtype), v).reshape(bsz, s, D_MODEL)
    return o @ wo

def setup_inputs(seed: int = 0) -> dict:
    key = jax.random.key(seed)
    ks = jax.random.split(key, 32)
    f32 = jnp.float32
    L, D = DEPTH, D_MODEL

    def nrm(k, shape, scale):
        return jax.random.normal(k, shape, f32) * scale

    def gain(k, shape):
        return 1.0 + 0.05 * jax.random.normal(k, shape, f32)

    return {
        "x": nrm(ks[0], (BATCH, SEQ, D), 1.0),
        "mem": nrm(ks[1], (BATCH, MEM_LEN, D), 1.0),
        "ffn1_norm": gain(ks[2], (L, D)),
        "ffn1_w_gate": nrm(ks[3], (L, D, D_FF), D ** -0.5),
        "ffn1_w_up": nrm(ks[4], (L, D, D_FF), D ** -0.5),
        "ffn1_w_down": nrm(ks[5], (L, D_FF, D), D_FF ** -0.5),
        "mix_norm": gain(ks[6], (L, D)),
        "w_in": nrm(ks[7], (L, D, D_IN_PROJ), D ** -0.5),
        "conv_w": nrm(ks[8], (L, CONV_K, CONV_WIDTH), CONV_K ** -0.5),
        "sg_norm": gain(ks[9], (L, SG_WIDTH)),
        "sg_w": nrm(ks[10], (L, SG_GROUPS, CHUNK, CHUNK), CHUNK ** -0.5),
        "sg_b": 1.0 + nrm(ks[11], (L, SG_GROUPS, CHUNK), 0.1),
        "fox_b_f": FORGET_BIAS_CENTER + nrm(ks[12], (L, FOX_HEADS), 1.0),
        "w_branch": nrm(ks[13], (L, N_BRANCH, BRANCH_WIDTH, D), BRANCH_WIDTH ** -0.5),
        "w_out": nrm(ks[14], (L, D, D), D ** -0.5),
        "xa_norm": gain(ks[15], (L, D)),
        "mem_norm": gain(ks[16], (L, D)),
        "xa_wq": nrm(ks[17], (L, D, D), D ** -0.5),
        "xa_wk": nrm(ks[18], (L, D, D), D ** -0.5),
        "xa_wv": nrm(ks[19], (L, D, D), D ** -0.5),
        "xa_wo": nrm(ks[20], (L, D, D), D ** -0.5),
        "ffn2_norm": gain(ks[21], (L, D)),
        "ffn2_w_gate": nrm(ks[22], (L, D, D_FF), D ** -0.5),
        "ffn2_w_up": nrm(ks[23], (L, D, D_FF), D ** -0.5),
        "ffn2_w_down": nrm(ks[24], (L, D_FF, D), D_FF ** -0.5),
        "final_norm": gain(ks[25], (D,)),
    }

def reference(x, mem, ffn1_norm, ffn1_w_gate, ffn1_w_up, ffn1_w_down, mix_norm, w_in,
              conv_w, sg_norm, sg_w, sg_b, fox_b_f, w_branch, w_out, xa_norm, mem_norm,
              xa_wq, xa_wk, xa_wv, xa_wo, ffn2_norm, ffn2_w_gate, ffn2_w_up, ffn2_w_down,
              final_norm):
    bsz, s, _ = x.shape
    split_idx = np.cumsum(SPLIT_SIZES)[:-1].tolist()
    for l in range(DEPTH):
        h = rmsnorm(x, ffn1_norm[l])
        x = x + 0.5 * swiglu(h, ffn1_w_gate[l], ffn1_w_up[l], ffn1_w_down[l])

        h = rmsnorm(x, mix_norm[l])
        proj = h @ w_in[l]
        (a_b, a_c, a_h, sg_u, sg_v, fq, fk, fv, f_logit, gate_logits) = jnp.split(
            proj, split_idx, axis=-1)
        y_a = short_conv_mixer(a_b, a_c, a_h, conv_w[l])
        y_b = spatial_gating_mixer(sg_u, sg_v, sg_norm[l], sg_w[l], sg_b[l])
        y_c = forgetting_attention(fq, fk, fv, f_logit, fox_b_f[l])
        branches = jnp.stack([y_a, y_b, y_c], axis=2)
        branches = jnp.einsum('bsnc,ncd->bsnd', branches, w_branch[l])
        gates = jax.nn.sigmoid(gate_logits.reshape(bsz, s, N_BRANCH, D_MODEL))
        merged = jnp.einsum('bsnd,bsnd->bsd', gates, branches)
        x = x + merged @ w_out[l]

        h = rmsnorm(x, xa_norm[l])
        m = rmsnorm(mem, mem_norm[l])
        x = x + memory_cross_attention(h, m, xa_wq[l], xa_wk[l], xa_wv[l], xa_wo[l])

        h = rmsnorm(x, ffn2_norm[l])
        x = x + 0.5 * swiglu(h, ffn2_w_gate[l], ffn2_w_up[l], ffn2_w_down[l])
    return rmsnorm(x, final_norm)


_drawn_inputs = setup_inputs


def setup_inputs(seed=0):
    import zlib

    import numpy as np

    out = dict(_drawn_inputs(seed))
    spreads = {}
    factors = {'sg_norm': 3.844, 'xa_norm': 8.0, 'mem_norm': 6.243, 'ffn2_norm': 3.042}
    for name, (base, spread) in spreads.items():
        noise = np.random.default_rng([zlib.crc32(name.encode()), seed]).standard_normal(out[name].shape)
        drawn = base * np.exp(spread * noise) if base else spread * noise
        out[name] = jnp.asarray(drawn.astype(out[name].dtype))
    for name, factor in factors.items():
        out[name] = (out[name] * factor).astype(out[name].dtype)
    return out
```

```python
import concourse.bass as bass
from concourse import mybir
from concourse.alu_op_type import AluOpType as ALU
from contextlib import ExitStack

F32 = mybir.dt.float32
F32R = mybir.dt.float32r
BF16 = mybir.dt.bfloat16
ACT = mybir.ActivationFunctionType
AX = mybir.AxisListType

LAYERS = 2
P = 128
T = 2
SEQ = T * P
D = 1024
KT = D // P
FF = 2816
FC = 256
STEPS = FF // FC
W5 = 512
UNIT = 2048
SLOTS = 3
HEADS, HD = 8, 64
XH = 4
GROUPS = 4
EPS = 1e-6
GATE = 440
FFN_UNITS = 3 * STEPS
NEG = -1e30

BLOCKS = [(n, [range(0, 4), range(4, 8)]) for n in
          ("fg", "q", "k", "v", "sv", "su", "ac", "ah", "ab", "g1", "g2", "g3", "g4", "g5", "g6")]
BLOCKS += [(n, [range(0, 4)]) for n in ("c0", "c1", "b0", "b1", "a0", "a1")]
BLOCKS += [("xk0", [range(0, 4), range(4, 8)]),
           ("wo0", [range(0, 3), range(3, 6), range(6, 8)]), ("wo1", [range(0, 4), range(4, 8)])]
BLOCKS += [(n, [range(0, 4), range(4, 8)]) for n in ("xk1", "xq0", "xq1", "xv0", "xv1", "xo0", "xo1")]
FIRST = {}
LAST = {}
_u = FFN_UNITS
for _n, _k in BLOCKS:
    FIRST[_n], LAST[_n] = _u, _u + len(_k) - 1
    _u += len(_k)
FFN_BASE = {1: 0, 2: _u}
UNITS = _u + FFN_UNITS
assert UNITS % SLOTS == 0 and FFN_BASE[2] % SLOTS == 0 and FFN_UNITS % SLOTS == 0
PAIR = {n: i % 2 for i, (n, _) in enumerate(BLOCKS)}
BEFORE = {n: BLOCKS[i - 2][0] for i, (n, _) in enumerate(BLOCKS) if i >= 2}

NPAR = 5 * KT + 12 + GROUPS
PAR = {"ffn1": 0, "mix": 8, "mem": 16, "xa": 24, "ffn2": 32, "conv": 40, "sgb": 52}
RMS = {"ffn1": 0, "mix": 1, "sv": 2, "mem": 3, "xa": 4, "ffn2": 5, "end": 6}


class Steps:

    def __init__(self, sem, names):
        self.sem, self.names = sem, names
        self.at_name = {n: i + 1 for i, n in enumerate(names)}
        assert len(self.at_name) == len(names)
        self.next = 0

    def done(self, layer, name, more=0):
        return layer * len(self.names) + (self.at_name[name] + more)

    def sign(self, instruction, name):
        assert self.names[self.next % len(self.names)] == name, (self.names[self.next % len(self.names)], name)
        self.next += 1
        return instruction.then_inc(self.sem, 1)

    def skip(self, n):
        self.next += n


def ffn_names(f, first, each, last):
    return [n(f, 0) for n in first] + [n(f, c) for c in range(1, STEPS) for n in each] + [n(f, STEPS - 1) for n in last]


def trunk(nc, weights, x_in, mem_in, params, sg_norm, sg_w, fox_b, final_g, out):
    ctx = ExitStack()
    with ctx:
        def sb(name, shape, dt=F32):
            return ctx.enter_context(nc.sbuf_tensor(name, shape, dt))

        def sem(name):
            return ctx.enter_context(nc.semaphore(name))

        raw = sb("raw", [P, SLOTS, UNIT])
        w_hi = sb("w_hi", [P, SLOTS, UNIT], F32R)
        w_lo = sb("w_lo", [P, SLOTS, UNIT], F32R)
        x = sb("x", [P, T, D])
        hg = sb("hg", [P, 2, W5])
        h_hi = sb("h_hi", [P, KT, SEQ], F32R)
        h_lo = sb("h_lo", [P, KT, SEQ], F32R)
        y_hi = sb("y_hi", [P, 12, SEQ], F32R)
        y_lo = sb("y_lo", [P, 12, SEQ], F32R)
        r1 = sb("r1", [P, 6144])
        r2 = sb("r2", [P, 7184])
        fg = sb("fg", [P, T, GATE])
        par = sb("par", [P, LAYERS, NPAR])
        sgn = sb("sgn", [P, LAYERS, W5])
        sgw_all = sb("sgw_all", [P, LAYERS, W5])
        sgw = sb("sgw", [P, W5])
        foxb = sb("foxb", [P, LAYERS, HEADS])
        junk = sb("junk", [P, D], BF16)
        ident = sb("ident", [P, P])
        ident_bf = sb("ident_bf", [P, P], BF16)
        mask_bf = sb("mask_bf", [P, P], BF16)
        head_row = sb("head_row", [HEADS, HEADS, P])
        neg_upper = sb("neg_upper", [P, SEQ])
        squares = sb("squares", [P, 7, T])
        eps = sb("eps", [P, T])
        meansq = sb("meansq", [P, 7, T])
        rms = sb("rms", [P, 7, T])
        half_power = sb("half_power", [P, T])
        lf = sb("lf", [P, 4, T, HEADS])
        neg_c = sb("neg_c", [HEADS, SEQ])
        neg_cq = sb("neg_cq", [P, T, HEADS])
        mx = sb("mx", [P, 3, HEADS])
        mxc = sb("mxc", [P, 3, HEADS])
        bias = sb("bias", [P, 3, HEADS])
        psums = sb("psums", [P, 3, HEADS])
        pinv = sb("pinv", [P, 3, HEADS])
        xmx = sb("xmx", [P, 2, 4])
        xbias = sb("xbias", [P, 2, 4])
        xsums = sb("xsums", [P, 2, 4])
        xinv = sb("xinv", [P, 2, 4])
        ps = ctx.enter_context(nc.psum_tensor("ps", [P, 8, W5], F32))

        def view(t, at, *shape):
            n = 1
            for s in shape:
                n *= s
            v = t[:, at:at + n]
            if len(shape) == 1:
                return v
            if len(shape) == 2:
                return v.rearrange("p (a b) -> p a b", b=shape[1])
            return v.rearrange("p (a b c) -> p a b c", b=shape[1], c=shape[2])

        silu = view(r1, 0, T, FC)
        glu = view(r1, 512, T, FC)
        glu_hi, glu_lo = y_hi[:, 0:2, :], y_lo[:, 0:2, :]
        p0 = view(r1, 0, HEADS, P)
        p1 = view(r1, 1024, HEADS, SEQ)
        pt0 = view(r1, 3072, HEADS, SEQ)
        pt1 = view(r1, 5120, HEADS, P)
        gates = view(r1, 0, T, 3 * D)
        q, k, v = view(r2, 0, T, W5), view(r2, 1024, T, W5), view(r2, 2048, T, W5)
        qt, kt = view(r2, 3072, 4, SEQ), view(r2, 4096, 4, SEQ)
        u, vb = view(r2, 5120, T, W5), view(r2, 6144, T, W5)
        az, ab = view(r2, 0, T, W5), view(r2, 1024, T, W5)
        zp = view(r2, 2048, 4, SEQ + 2)
        ya = view(r2, 4096, 4, SEQ)
        merged = view(r2, 5120, T, D)
        gated = view(r2, 0, 4, W5)
        mem = view(r2, 2048, T, D)
        m_hi, m_lo = y_hi[:, 0:KT, :], y_lo[:, 0:KT, :]
        xkt, xqt, xv = view(r1, 0, KT, SEQ), view(r1, 2048, KT, SEQ), view(r1, 4096, T, D)
        xk = view(r2, 0, T, W5)
        xq = [view(r2, 1024, T, W5), view(r2, 2048, T, W5)]
        xp = [view(r2, 3072, T, W5), view(r2, 4096, T, W5)]
        xpt = view(r2, 5120, XH, T, SEQ)

        hg_out = view(r1, 0, T, D)
        final_gain = view(r1, 2048, D)

        raw_loaded = [sem(f"raw_loaded{i}") for i in range(SLOTS)]
        inputs_loaded = sem("inputs_loaded")
        consts_loaded = sem("consts_loaded")
        mem_loaded = sem("mem_loaded")
        consts_made = sem("consts_made")
        hi_split = Steps(sem("hi_split"), list(range(UNITS)))
        lo_split = Steps(sem("lo_split"), list(range(UNITS)))
        unit_used = Steps(sem("unit_used"), list(range(UNITS)))
        out_stored = sem("out_stored")
        ended = sem("ended")

        TH1 = [(0, 0), (0, 1), (1, 0), (1, 1)]
        TH2 = [(0, 0), (1, 0), (0, 1), (1, 1)]
        TURNS = {"ffn1": TH1, "mix": TH1, "mem": TH1, "mg": TH1, "xa": TH2, "ffn2": TH2}

        def th(kind, stage):
            return [(kind, stage, t, h) for t, h in TURNS[stage]]

        def gu(f, c):
            return ("gu", f, c)

        acc_done = Steps(sem("acc_done"),
                         [gu(1, c) for c in range(STEPS)] + [("down", 1)] + [n for n, _ in BLOCKS]
                         + [gu(2, c) for c in range(STEPS)] + [("down", 2)])
        turned = Steps(sem("turned"),
                       th("t", "ffn1") + [("glu", 1, c) for c in range(STEPS)] + th("t", "mix")
                       + ["q", "k", "p0", "p1", "p2", "z", "ab", "yb"] + th("t", "mem") + th("t", "mg")
                       + ["xk0"] + th("t", "xa") + ["xk1", "xq0", "xq1", "xpa", "xpb"]
                       + th("t", "ffn2") + [("glu", 2, c) for c in range(STEPS)])
        mixed = Steps(sem("mixed"), ["c", "s0", "s1", "s2", "pv", "sg", "xsa", "xsb", "xva", "xvb"])

        def act_ffn(f):
            return [("silu", f, 0, 0), ("silu", f, 0, 1)] + \
                [s for c in range(1, STEPS) for s in (("gluhi", f, c - 1), ("silu", f, c, 0), ("silu", f, c, 1))] + \
                [("gluhi", f, STEPS - 1)]

        def sq(stage):
            return [("sq", stage, 0), ("sq", stage, 1)]

        act_done = Steps(sem("act_done"),
                         th("hi", "ffn1") + sq("ffn1") + act_ffn(1) + th("hi", "mix") + sq("mix")
                         + [("fg", 0), ("fg", 1), "exp", "ln", ("q", 0), ("q", 1), "negc", "negcq",
                            ("k", 0), ("k", 1), "qt", ("v", 0), ("v", 1), "kt",
                            "e0", ("sv", 0), ("sv", 1)] + sq("sv")
                         + [("su", 0), ("su", 1), "e1", "e2", ("ac", 0), ("ac", 1), "pt0", "pt1", "pt2",
                            "ychi", ("ab", 0), ("ab", 1), "zp", ("g0", 0), ("g0", 1), ("g1", 0), ("g1", 1),
                            "ybhi", ("g2", 0), ("g2", 1), "yahi"]
                         + [(g, t) for g in ("g3", "g4", "g5", "g6") for t in range(T)]
                         + sq("mem") + th("hi", "mem") + th("hi", "mg") + [("xk0", 0), ("xk0", 1), "xkt0"]
                         + th("hi", "xa") + sq("xa") + [("xk1", 0), ("xk1", 1), ("xq0", 0), ("xq0", 1), "xkt1", "xqt0",
                            ("xq1", 0), ("xq1", 1), "xea", "xqt1", ("xv0", 0), ("xv0", 1), "xeb", "xpt0",
                            ("xv1", 0), ("xv1", 1), "xpt1", "oahi", "obhi"]
                         + th("hi", "ffn2") + sq("ffn2") + act_ffn(2))

        def dve_ffn(f):
            return [("mul", f, 0, 0), ("mul", f, 0, 1)] + \
                [s for c in range(1, STEPS) for s in (("glulo", f, c - 1), ("mul", f, c, 0), ("mul", f, c, 1))] + \
                [("glulo", f, STEPS - 1)]

        def xn(stage, order):
            return [("x", stage, t, h) for t, h in order]

        def norm_dve(stage, t, h):
            return [("hg", stage, t, h), ("lo", stage, t, h)]

        dve_done = Steps(sem("dve_done"),
                         [s for t, h in TH1 for s in norm_dve("ffn1", t, h)] + dve_ffn(1)
                         + [s for t in range(T) for s in [("x", "f1", t, 0), ("x", "f1", t, 1)]
                            + norm_dve("mix", t, 0) + norm_dve("mix", t, 1)]
                         + ["z", "az", "logf", "mx0", "mxc0", "bias0", ("vb", 0), ("vb", 1), "inv0", "pn0",
                            "mx1", "mxc1", "bias1", "inv1", "pn1", "mx2", "mxc2", "bias2", "inv2", "pn2",
                            ("az", 0), ("az", 1), "pad", "yclo", ("yb", 0), ("yb", 1), "conv", "ya", "yblo", "yalo"]
                         + [(b, t) for b in ("c0", "c1", "b0", "b1") for t in range(T)]
                         + [s for t, h in TH1 for s in norm_dve("mem", t, h)]
                         + [(b, t) for b in ("a0", "a1") for t in range(T)]
                         + th("lo", "mg") + xn("wo", [(0, 0), (1, 0)])
                         + norm_dve("xa", 0, 0) + norm_dve("xa", 1, 0) + xn("wo", [(0, 1), (1, 1)])
                         + norm_dve("xa", 0, 1) + norm_dve("xa", 1, 1)
                         + ["xmxa", "xbiasa", "xinva", "xpna", "xmxb", "xbiasb", "xinvb", "xpnb", "oalo", "oblo"]
                         + xn("xo", [(0, 0), (1, 0)]) + norm_dve("ffn2", 0, 0) + norm_dve("ffn2", 1, 0)
                         + xn("xo", [(0, 1), (1, 1)]) + norm_dve("ffn2", 0, 1) + norm_dve("ffn2", 1, 1)
                         + dve_ffn(2)
                         + [("x", "f2", t, h) for t, h in TH1])
        conv_chain = Steps(sem("conv_chain"), [("conv", i, c) for i in range(2) for c in range(4)])
        pool_done = Steps(sem("pool_done"),
                          ["sgw"] + [(m, s) for s in ("ffn1", "mix", "sv", "mem") for m in ("mean", "rms")]
                          + [("add", b, t) for b in ("b0", "b1", "a0", "a1") for t in range(T)]
                          + [(m, s) for s in ("xa", "ffn2") for m in ("mean", "rms")])

        block = ctx.enter_context(nc.Block())

        @block.sync
        def _(sp):
            for s in range(SLOTS):
                sp.dma_start(raw[:, s, :], weights[s, :, :]).then_inc(raw_loaded[s], 16)
            with sp.Fori(1, LAYERS * UNITS // SLOTS) as turn:
                for s in range(SLOTS):
                    sp.wait_ge(lo_split.sem, (turn - 1) * SLOTS + (s + 1))
                    sp.dma_start(raw[:, s, :], weights[turn * SLOTS + s, :, :]).then_inc(raw_loaded[s], 16)
            for t in range(T):
                sp.wait_ge(ended, 5 + t)
                sp.dma_start(out[t * P:(t + 1) * P, :], hg_out[:, t, :]).then_inc(out_stored, 16)
            sp.wait_ge(out_stored, 32)

        @block.gpsimd
        def _(pool):
            pool.dma_start(x[:, :, :], x_in.rearrange("(t p) d -> p t d", p=P)).then_inc(inputs_loaded, 16)
            pool.dma_start(par[:, :, :], params.rearrange("l p n -> p l n")).then_inc(consts_loaded, 16)
            for l in range(LAYERS):
                pool.dma_start(sgn[:, l, :], sg_norm[l:l + 1, :].to_broadcast([P, W5])).then_inc(consts_loaded, 16)
                pool.dma_start(foxb[:, l, :], fox_b[l:l + 1, :].to_broadcast([P, HEADS])).then_inc(consts_loaded, 16)
                pool.dma_start(sgw_all[:, l, :], sg_w[l, :, :]).then_inc(consts_loaded, 16)
            nc.gpsimd.memset(ident[:, :], 0.0).then_inc(consts_made, 1)
            nc.gpsimd.memset(mask_bf[:, :], 0.0).then_inc(consts_made, 1)
            nc.gpsimd.memset(head_row[:, :, :], 0.0).then_inc(consts_made, 1)
            nc.gpsimd.memset(neg_upper[:, :], -1.0).then_inc(consts_made, 1)
            nc.gpsimd.memset(half_power[:, :], -0.5).then_inc(consts_made, 1)
            nc.gpsimd.memset(eps[:, :], EPS).then_inc(consts_made, 1)
            pool.wait_ge(consts_made, 6)
            nc.gpsimd.affine_select(out=ident[:, :], in_=ident[:, :], compare_op=ALU.not_equal, fill=1.0, base=0,
                                    pattern=[[-1, P]], channel_multiplier=1).then_inc(consts_made, 1)
            nc.gpsimd.affine_select(out=mask_bf[:, :], in_=mask_bf[:, :], compare_op=ALU.is_ge, fill=NEG, base=0,
                                    pattern=[[-1, P]], channel_multiplier=1).then_inc(consts_made, 1)
            nc.gpsimd.affine_select(out=head_row[:, :, :], in_=head_row[:, :, :], compare_op=ALU.not_equal, fill=1.0,
                                    base=0, pattern=[[-1, HEADS], [0, P]], channel_multiplier=1).then_inc(consts_made, 1)
            nc.gpsimd.affine_select(out=neg_upper[:, 0:P], in_=neg_upper[:, 0:P], compare_op=ALU.is_ge, fill=0.0,
                                    base=0, pattern=[[1, P]], channel_multiplier=-1).then_inc(consts_made, 1)
            pool.wait_ge(consts_made, 7)
            nc.gpsimd.tensor_copy(ident_bf[:, :], ident[:, :]).then_inc(consts_made, 1)
            pool.wait_ge(consts_loaded, 16 * (1 + 3 * LAYERS))
            for l in range(LAYERS):
                sw = sgw_all[:, l, :].rearrange("p (g t) -> p g t", g=GROUPS)
                nc.gpsimd.affine_select(out=sw, in_=sw, compare_op=ALU.is_ge, fill=0.0, base=0,
                                        pattern=[[0, GROUPS], [1, P]], channel_multiplier=-1).then_inc(consts_made, 1)

            def inverse_rms(L, stage, last_square):
                i = RMS[stage]
                pool.wait_ge(act_done.sem, last_square)
                m = nc.gpsimd.tensor_tensor(meansq[:, i, :], squares[:, i, :], eps[:, :], ALU.add)
                if stage == "end":
                    m.then_inc(ended, 1)
                    pool.wait_ge(ended, 3)
                else:
                    pool_done.sign(m, ("mean", stage))
                    pool.wait_ge(pool_done.sem, pool_done.done(L, ("mean", stage)))
                r = nc.gpsimd.tensor_tensor(rms[:, i, :], meansq[:, i, :], half_power[:, :], ALU.pow)
                return r.then_inc(ended, 1) if stage == "end" else pool_done.sign(r, ("rms", stage))

            pool.wait_ge(consts_made, 11 + LAYERS)
            with pool.Fori(0, LAYERS) as L:
                pool_done.sign(nc.gpsimd.tensor_copy(sgw[:, :], sgw_all[:, L, :]), "sgw")
                for stage in ("ffn1", "mix", "sv"):
                    inverse_rms(L, stage, act_done.done(L, ("sq", stage, 1)))
                inverse_rms(L, "mem", act_done.done(L, ("sq", "mem", 1)))
                slot = 0
                for b in ("b0", "b1", "a0", "a1"):
                    half = int(b[1])
                    for t in range(T):
                        pool.wait_ge(dve_done.sem, dve_done.done(L, (b, t)))
                        if b[0] == "a":
                            pool.wait_ge(pool_done.sem, pool_done.done(L, ("add", "b" + b[1], t)))
                        m = merged[:, t, half * W5:(half + 1) * W5]
                        pool_done.sign(nc.gpsimd.tensor_tensor(m, m, gated[:, slot % 4, :], ALU.add), ("add", b, t))
                        slot += 1
                inverse_rms(L, "xa", act_done.done(L, ("sq", "xa", 1)))
                inverse_rms(L, "ffn2", act_done.done(L, ("sq", "ffn2", 1)))
            pool.wait_ge(act_done.sem, LAYERS * len(act_done.names))
            pool.wait_ge(turned.sem, LAYERS * len(turned.names))
            pool.dma_start(final_gain, final_g.to_broadcast([P, D])).then_inc(consts_loaded, 16)
            pool.wait_ge(ended, 2)
            inverse_rms(0, "end", 1)

        @block.scalar
        def _(act):
            def hi(L, n):
                s = n % SLOTS
                act.wait_ge(raw_loaded[s], L * (16 * UNITS // SLOTS) + 16 * (n // SLOTS + 1))
                hi_slot(L, n, s)

            def hi_slot(L, n, s, more=0):
                if free_first(n):
                    act.wait_ge(unit_used.sem, unit_used.done(L, n - SLOTS, more))
                hi_split.sign(nc.scalar.copy(w_hi[:, s, :], raw[:, s, :]), n)

            def free_first(n):
                return n >= SLOTS

            def hi_first(L, n):
                hi(L, n)

            def result(L, name, t):
                if t == 0:
                    act.wait_ge(acc_done.sem, acc_done.done(L, name))
                else:
                    act.wait_ge(unit_used.sem, unit_used.done(L, LAST[name]))

            def rms_ready(L, stage):
                act.wait_ge(pool_done.sem, pool_done.done(L, ("rms", stage)))

            def take(L, name, t, out_ap, stage, func=ACT.Copy, cols=slice(0, W5)):
                result(L, name, t)
                b = 2 * PAIR[name] + t
                act_done.sign(nc.scalar.activation(out_ap, ps[:, b, cols], func,
                                                   scale=rms[:, RMS[stage], t:t + 1]),
                              (name, t))

            def split_norm(L, stage, t, h, hi_ap):
                act.wait_ge(dve_done.sem, dve_done.done(L, ("hg", stage, t, h)))
                n = TURNS[stage].index((t, h)) % 2
                act_done.sign(nc.scalar.copy(hi_ap[:, 4 * h:4 * h + 4, t * P:(t + 1) * P],
                                             hg[:, n, :].rearrange("p (k s) -> p k s", k=4)), ("hi", stage, t, h))

            def square(L, stage, t, src, width):
                if t == 1:
                    if stage == "end":
                        act.wait_ge(ended, 1)
                    else:
                        act.wait_ge(act_done.sem, act_done.done(L, ("sq", stage, 0)))
                return nc.scalar.activation(junk[:, 0:width], src, ACT.Square,
                                            scale=width ** -0.5, accum_out=squares[:, RMS[stage], t:t + 1])

            def ffn(L, f):
                base = FFN_BASE[f]
                stage = f"ffn{f}"

                def silus(c, more_a=0, more_u=0):
                    for t in range(T):
                        if t == 0:
                            act.wait_ge(acc_done.sem, acc_done.done(L, gu(f, min(c, 2)), more_a))
                        else:
                            act.wait_ge(unit_used.sem, unit_used.done(L, base + (1 if c == 0 else 3 * min(c, 2)), more_u))
                        if c == 0 and t == 0:
                            rms_ready(L, stage)
                        if c > 0:
                            act.wait_ge(dve_done.sem, dve_done.done(L, ("mul", f, min(c, 2) - 1, t), 3 * more_a))
                        act_done.sign(nc.scalar.activation(silu[:, t, :], ps[:, t, 0:FC], ACT.Silu,
                                                           scale=rms[:, RMS[stage], t:t + 1]), ("silu", f, min(c, 2), t))

                def glu_split(c, more=0):
                    act.wait_ge(turned.sem, turned.done(L, ("glu", f, c), more))
                    if c > 0:
                        act.wait_ge(unit_used.sem, unit_used.done(L, base + 3 * c + 1, 3 * more))
                    act_done.sign(nc.scalar.copy(glu_hi, ps[:, 2, :].rearrange("p (k s) -> p k s", k=2)), ("gluhi", f, c))

                def step(c, more=0):
                    for i in range(3):
                        if i == 1:
                            glu_split(c - 1, more)
                        n = base + 3 * c + i
                        act.wait_ge(raw_loaded[i], L * (16 * UNITS // SLOTS) + (16 * ((base + 3 * c) // SLOTS + 1) + 16 * more))
                        act.wait_ge(unit_used.sem, unit_used.done(L, n - SLOTS, 3 * more))
                        hi_split.sign(nc.scalar.copy(w_hi[:, i, :], raw[:, i, :]), n)
                    silus(c, more, 3 * more)

                silus(0)
                step(1)
                with act.Fori(0, STEPS - 2) as more:
                    step(2, more)
                hi_split.skip(3 * (STEPS - 3))
                act_done.skip(3 * (STEPS - 3))
                glu_split(STEPS - 1)

            act.wait_ge(inputs_loaded, 16)
            with act.Fori(0, LAYERS) as L:
                hi_first(L, 0)
                hi_first(L, 1)
                for t, h in TH1:
                    split_norm(L, "ffn1", t, h, h_hi)
                hi_first(L, 2)
                for t in range(T):
                    act_done.sign(square(L, "ffn1", t, x[:, t, :], D), ("sq", "ffn1", t))
                ffn(L, 1)
                hi(L, 33)
                hi(L, 34)
                for t, h in TH1:
                    split_norm(L, "mix", t, h, h_hi)
                hi(L, 35)
                for t in range(T):
                    act_done.sign(square(L, "mix", t, x[:, t, :], D), ("sq", "mix", t))
                hi(L, 36)
                rms_ready(L, "mix")
                for t in range(T):
                    take(L, "fg", t, fg[:, t, :], "mix", cols=slice(0, GATE))
                hi(L, 37)
                act.wait_ge(dve_done.sem, dve_done.done(L, "az"))
                act_done.sign(nc.scalar.activation(lf[:, 1, :, :], lf[:, 1, :, :], ACT.Exp, scale=-1.0), "exp")
                act.wait_ge(act_done.sem, act_done.done(L, "exp"))
                act_done.sign(nc.scalar.activation(lf[:, 2, :, :], lf[:, 1, :, :], ACT.Ln, bias=1.0), "ln")
                hi(L, 38)
                for t in range(T):
                    take(L, "q", t, q[:, t, :], "mix")
                act.wait_ge(mixed.sem, mixed.done(L, "c"))
                act_done.sign(nc.scalar.copy(neg_c[:, :], ps[0:HEADS, 7, 0:SEQ]), "negc")
                act_done.sign(nc.scalar.copy(neg_cq[:, :, :], ps[:, 7, SEQ:SEQ + 16].rearrange("p (t h) -> p t h", t=T)), "negcq")
                hi(L, 39)
                hi(L, 40)
                for t in range(T):
                    take(L, "k", t, k[:, t, :], "mix")
                act.wait_ge(turned.sem, turned.done(L, "q"))
                act_done.sign(nc.scalar.mul(qt, ps[:, 4:6, :].rearrange("p b (c s) -> p (b c) s", c=2), HD ** -0.5), "qt")
                hi(L, 41)
                hi(L, 42)
                for t in range(T):
                    take(L, "v", t, v[:, t, :], "mix")
                act.wait_ge(turned.sem, turned.done(L, "k"))
                act_done.sign(nc.scalar.copy(kt, ps[:, 6:8, :].rearrange("p b (c s) -> p (b c) s", c=2)), "kt")
                hi(L, 43)
                hi(L, 44)

                def exps(L, part, n, tile, name):
                    act.wait_ge(dve_done.sem, dve_done.done(L, f"bias{part}"))
                    bank, width = {0: (4, P), 1: (6, SEQ), 2: (4, SEQ)}[part]
                    for i in range(n):
                        h = i + (4 if part == 2 else 0)
                        o = p0[:, h, :] if part == 0 else p1[:, h, :]
                        e = nc.scalar.activation(o, ps[:, bank + i % 2, i // 2 * width:(i // 2 + 1) * width], ACT.Exp,
                                                 bias=bias[:, part, i:i + 1], accum_out=psums[:, part, i:i + 1])
                    act_done.sign(e, name)

                exps(L, 0, HEADS, 0, "e0")
                hi(L, 45)
                for t in range(T):
                    take(L, "sv", t, vb[:, t, :], "mix", ACT.Gelu_apprx_tanh)
                for t in range(T):
                    act.wait_ge(act_done.sem, act_done.done(L, ("sv", t)))
                    act_done.sign(square(L, "sv", t, vb[:, t, :], W5), ("sq", "sv", t))
                hi(L, 46)
                for t in range(T):
                    take(L, "su", t, u[:, t, :], "mix", ACT.Gelu_apprx_tanh)
                exps(L, 1, 4, 1, "e1")
                hi(L, 47)
                exps(L, 2, 4, 1, "e2")
                hi(L, 48)
                for t in range(T):
                    take(L, "ac", t, az[:, t, :], "mix")

                def probs_out(L, name, where, bank):
                    act.wait_ge(turned.sem, turned.done(L, name))
                    act_done.sign(nc.scalar.copy(where, ps[:, bank:bank + 2, :].rearrange(
                        "p b (c s) -> p (b c) s", s=where.shape[-1])), {"p0": "pt0", "p1": "pt1", "p2": "pt2"}[name])

                probs_out(L, "p0", pt0[:, 0:4, :], 6)
                hi(L, 49)
                probs_out(L, "p1", pt0[:, 4:8, :], 4)
                hi(L, 50)
                probs_out(L, "p2", pt1, 6)
                hi(L, 51)
                act.wait_ge(mixed.sem, mixed.done(L, "pv"))
                act_done.sign(nc.scalar.copy(y_hi[:, 0:4, :], ps[:, 4:6, :].rearrange("p b (c s) -> p (b c) s", c=2)), "ychi")
                hi(L, 52)
                for t in range(T):
                    take(L, "ab", t, ab[:, t, :], "mix")
                hi(L, 53)
                act.wait_ge(turned.sem, turned.done(L, "z"))
                act_done.sign(nc.scalar.copy(zp[:, :, 2:SEQ + 2], ps[:, 4:6, :].rearrange("p b (c s) -> p (b c) s", c=2)), "zp")
                for t in range(T):
                    act_done.sign(nc.scalar.activation(gates[:, t, 0:GATE - HEADS], fg[:, t, HEADS:GATE], ACT.Sigmoid),
                                  ("g0", t))
                hi(L, 54)

                def gate(L, i):
                    at = GATE * i - HEADS
                    for t in range(T):
                        take(L, f"g{i}", t, gates[:, t, at:at + GATE], "mix", ACT.Sigmoid, cols=slice(0, GATE))

                gate(L, 1)
                hi(L, 55)
                act.wait_ge(turned.sem, turned.done(L, "yb"))
                act_done.sign(nc.scalar.copy(y_hi[:, 4:8, :], ps[:, 4:6, :].rearrange("p b (c s) -> p (b c) s", c=2)), "ybhi")
                hi(L, 56)
                gate(L, 2)
                act.wait_ge(dve_done.sem, dve_done.done(L, "ya"))
                act.dma_start(mem, mem_in.rearrange("(t p) d -> p t d", p=P)).then_inc(mem_loaded, 16)
                act_done.sign(nc.scalar.copy(y_hi[:, 8:12, :], ya), "yahi")
                hi(L, 57)
                hi(L, 58)
                for i in (3, 4, 5, 6):
                    gate(L, i)
                    hi(L, 59 + 2 * (i - 3))
                    if i < 6:
                        hi(L, 60 + 2 * (i - 3))
                act.wait_ge(mem_loaded, L * 16 + 16)
                for t in range(T):
                    act_done.sign(square(L, "mem", t, mem[:, t, :], D), ("sq", "mem", t))
                hi(L, 66)
                hi(L, 67)
                hi(L, 68)
                for t, h in TH1:
                    split_norm(L, "mem", t, h, m_hi)
                hi(L, 69)
                hi(L, 70)
                hi(L, 71)
                for t, h in TH1:
                    act.wait_ge(turned.sem, turned.done(L, ("t", "mg", t, h)))
                    act_done.sign(nc.scalar.copy(h_hi[:, 4 * h:4 * h + 4, t * P:(t + 1) * P],
                                                 ps[:, 4 + 2 * t + h, :].rearrange("p (k s) -> p k s", k=4)),
                                  ("hi", "mg", t, h))
                hi(L, 72)
                rms_ready(L, "mem")
                for t in range(T):
                    take(L, "xk0", t, xk[:, t, :], "mem")
                hi(L, 73)
                hi(L, 74)

                def turned_out(L, name, what, where, bank, scale=1.0):
                    act.wait_ge(turned.sem, turned.done(L, name))
                    act_done.sign(nc.scalar.mul(where, ps[:, bank:bank + 2, :].rearrange("p b (c s) -> p (b c) s", c=2), scale), what)

                turned_out(L, "xk0", "xkt0", xkt[:, 0:4, :], 4)
                hi(L, 75)
                hi(L, 76)
                hi(L, 77)
                for t, h in TH2[0:2]:
                    split_norm(L, "xa", t, h, h_hi)
                hi(L, 78)
                for t, h in TH2[2:4]:
                    split_norm(L, "xa", t, h, h_hi)
                hi(L, 79)
                for t in range(T):
                    act_done.sign(square(L, "xa", t, x[:, t, :], D), ("sq", "xa", t))
                for t in range(T):
                    take(L, "xk1", t, xk[:, t, :], "mem")
                hi(L, 80)
                hi(L, 81)
                rms_ready(L, "xa")
                for t in range(T):
                    take(L, "xq0", t, xq[0][:, t, :], "xa")
                turned_out(L, "xk1", "xkt1", xkt[:, 4:8, :], 4)
                hi(L, 82)
                turned_out(L, "xq0", "xqt0", xqt[:, 0:4, :], 6, (D // XH) ** -0.5)
                hi(L, 83)
                for t in range(T):
                    take(L, "xq1", t, xq[1][:, t, :], "xa")

                def xexps(L, part, name):
                    act.wait_ge(dve_done.sem, dve_done.done(L, "xbias" + "ab"[part]))
                    for i in range(4):
                        t, h = i // 2, i % 2
                        e = nc.scalar.activation(xp[part][:, t, h * SEQ:(h + 1) * SEQ],
                                                 ps[:, 4 + t, h * SEQ:(h + 1) * SEQ], ACT.Exp,
                                                 bias=xbias[:, part, i:i + 1], accum_out=xsums[:, part, i:i + 1])
                    act_done.sign(e, name)

                xexps(L, 0, "xea")
                hi(L, 84)
                turned_out(L, "xq1", "xqt1", xqt[:, 4:8, :], 6, (D // XH) ** -0.5)
                hi(L, 85)
                for t in range(T):
                    take(L, "xv0", t, xv[:, t, 0:W5], "mem")
                xexps(L, 1, "xeb")
                hi(L, 86)
                act.wait_ge(turned.sem, turned.done(L, "xpa"))
                act_done.sign(nc.scalar.copy(xpt[:, 0:2, :, :].rearrange("p h k s -> p (h k s)"),
                                             ps[:, 6:8, :].rearrange("p b s -> p (b s)")), "xpt0")
                hi(L, 87)
                for t in range(T):
                    take(L, "xv1", t, xv[:, t, W5:D], "mem")
                act.wait_ge(turned.sem, turned.done(L, "xpb"))
                act_done.sign(nc.scalar.copy(xpt[:, 2:4, :, :].rearrange("p h k s -> p (h k s)"),
                                             ps[:, 4:6, :].rearrange("p b s -> p (b s)")), "xpt1")
                for half, (m, bank) in enumerate((("xva", 6), ("xvb", 4))):
                    act.wait_ge(mixed.sem, mixed.done(L, m))
                    act_done.sign(nc.scalar.copy(h_hi[:, 4 * half:4 * half + 4, :],
                                                 ps[:, bank:bank + 2, :].rearrange("p b (c s) -> p (b c) s", c=2)),
                                  ("oahi", "obhi")[half])
                hi(L, 88)
                hi(L, 89)
                hi(L, 90)
                for t, h in TH2[0:2]:
                    split_norm(L, "ffn2", t, h, h_hi)
                hi(L, 91)
                for t, h in TH2[2:4]:
                    split_norm(L, "ffn2", t, h, h_hi)
                hi(L, 92)
                for t in range(T):
                    act_done.sign(square(L, "ffn2", t, x[:, t, :], D), ("sq", "ffn2", t))
                ffn(L, 2)
                act.wait_ge(dve_done.sem, dve_done.done(L, ("x", "f2", 1, 1)))
            for t in range(T):
                square(0, "end", t, x[:, t, :], D).then_inc(ended, 1)

        @block.vector
        def _(dve):
            def lo_of(n, s):
                return lo_split.sign(nc.vector.tensor_tensor(w_lo[:, s, :], raw[:, s, :], w_hi[:, s, :].bitcast(F32),
                                                             ALU.subtract), n)

            def lo(L, n):
                dve.wait_ge(hi_split.sem, hi_split.done(L, n))
                lo_of(n, n % SLOTS)

            def result(L, name, t):
                if t == 0:
                    dve.wait_ge(acc_done.sem, acc_done.done(L, name))
                else:
                    dve.wait_ge(unit_used.sem, unit_used.done(L, LAST[name]))

            def gain(L, stage):
                at = PAR[stage]
                return par[:, L, at:at + KT]

            def normed(L, stage, t, h, lo_ap):
                n = TURNS[stage].index((t, h)) % 2
                at = PAR[stage] + 4 * h
                dve.wait_ge(turned.sem, turned.done(L, ("t", stage, t, h)))
                if TURNS[stage].index((t, h)) >= 2:
                    before = TURNS[stage][TURNS[stage].index((t, h)) - 2]
                    dve.wait_ge(dve_done.sem, dve_done.done(L, ("lo", stage) + before))
                g = par[:, L, at:at + 4].rearrange("p (k s) -> p k s", s=1).to_broadcast([P, 4, P])
                o = hg[:, n, :].rearrange("p (k s) -> p k s", k=4)
                dve_done.sign(nc.vector.tensor_tensor(o, ps[:, 4 + 2 * t + h, :].rearrange("p (k s) -> p k s", k=4),
                                                      g, ALU.mult), ("hg", stage, t, h))
                dve.wait_ge(act_done.sem, act_done.done(L, ("hi", stage, t, h)))
                hi_ap = {id(h_lo): h_hi, id(y_lo): y_hi}[id(lo_ap)]
                cut = (slice(None), slice(4 * h, 4 * h + 4), slice(t * P, (t + 1) * P))
                dve_done.sign(nc.vector.tensor_tensor(lo_ap[cut], o, hi_ap[cut].bitcast(F32), ALU.subtract),
                              ("lo", stage, t, h))

            def add_down(L, f, t):
                for h in range(2):
                    if t == 0:
                        dve.wait_ge(acc_done.sem, acc_done.done(L, ("down", f)))
                    else:
                        dve.wait_ge(unit_used.sem, unit_used.done(L, FFN_BASE[f] + FFN_UNITS - 1))
                    xs = x[:, t, h * W5:(h + 1) * W5]
                    dve_done.sign(nc.vector.scalar_tensor_tensor(out=xs, in0=ps[:, 4 + 2 * t + h, :], scalar=0.5, in1=xs,
                                                                 op0=ALU.mult, op1=ALU.add), ("x", f"f{f}", t, h))

            def add_block(L, name, what, t, h):
                result(L, name, t)
                xs = x[:, t, h * W5:(h + 1) * W5]
                dve_done.sign(nc.vector.tensor_tensor(xs, ps[:, 2 * PAIR[name] + t, :], xs, ALU.add), ("x", what, t, h))

            def ffn(L, f):
                base = FFN_BASE[f]
                i_rms = RMS[f"ffn{f}"]

                def muls(c, more=0):
                    for t in range(T):
                        dve.wait_ge(act_done.sem, act_done.done(L, ("silu", f, c, t), 3 * more))
                        if c > 0:
                            dve.wait_ge(turned.sem, turned.done(L, ("glu", f, c - 1), more))
                        dve_done.sign(nc.vector.scalar_tensor_tensor(
                            out=glu[:, t, :], in0=ps[:, t, FC:2 * FC], scalar=rms[:, i_rms, t:t + 1], in1=silu[:, t, :],
                            op0=ALU.mult, op1=ALU.mult), ("mul", f, c, t))

                def glu_split(c, more=0):
                    dve.wait_ge(act_done.sem, act_done.done(L, ("gluhi", f, c), 3 * more))
                    dve_done.sign(nc.vector.tensor_tensor(glu_lo, ps[:, 2, :].rearrange("p (k s) -> p k s", k=2),
                                                          glu_hi.bitcast(F32), ALU.subtract), ("glulo", f, c))

                def step(c, more=0):
                    for i in range(3):
                        if i == 1:
                            glu_split(c - 1, more)
                        n = base + 3 * c + i
                        dve.wait_ge(hi_split.sem, hi_split.done(L, n, 3 * more))
                        lo_of(n, i)
                    muls(c, more)

                muls(0)
                step(1)
                with dve.Fori(0, STEPS - 2) as more:
                    step(2, more)
                lo_split.skip(3 * (STEPS - 3))
                dve_done.skip(3 * (STEPS - 3))
                glu_split(STEPS - 1)

            dve.wait_ge(consts_loaded, 16 * (1 + 3 * LAYERS))
            dve.wait_ge(inputs_loaded, 16)
            with dve.Fori(0, LAYERS) as L:
                lo(L, 0)
                lo(L, 1)
                for t, h in TH1:
                    normed(L, "ffn1", t, h, h_lo)
                lo(L, 2)
                ffn(L, 1)
                lo(L, 33)
                lo(L, 34)
                for t in range(T):
                    add_down(L, 1, t)
                    normed(L, "mix", t, 0, h_lo)
                    normed(L, "mix", t, 1, h_lo)
                lo(L, 35)
                lo(L, 36)
                dve.wait_ge(act_done.sem, act_done.done(L, ("fg", 1)))
                dve_done.sign(nc.vector.tensor_tensor(lf[:, 0, :, :], fg[:, :, 0:HEADS],
                                                      foxb[:, L, :].rearrange("p (a h) -> p a h", a=1).to_broadcast([P, T, HEADS]),
                                                      ALU.add), "z")
                dve.wait_ge(dve_done.sem, dve_done.done(L, "z"))
                dve_done.sign(nc.vector.scalar_tensor_tensor(out=lf[:, 1, :, :], in0=lf[:, 0, :, :], scalar=-1.0,
                                                             in1=lf[:, 0, :, :], op0=ALU.mult, op1=ALU.max), "az")
                lo(L, 37)
                dve.wait_ge(act_done.sem, act_done.done(L, "ln"))
                dve_done.sign(nc.vector.scalar_tensor_tensor(out=lf[:, 3, :, :], in0=lf[:, 0, :, :], scalar=0.0,
                                                             in1=lf[:, 2, :, :], op0=ALU.min, op1=ALU.subtract), "logf")
                for n in range(38, 45):
                    lo(L, n)

                def maxima(L, part):
                    dve.wait_ge(mixed.sem, mixed.done(L, f"s{part}"))
                    bank, width, n = {0: (4, P, 8), 1: (6, SEQ, 4), 2: (4, SEQ, 4)}[part]
                    tile, first = (0, 0) if part == 0 else (1, 0 if part == 1 else 4)
                    dve_done.sign(nc.vector.reduce_max(mx[:, part, 0:n].rearrange("p (c b) -> p b c", b=2),
                                                       ps[:, bank:bank + 2, :].rearrange("p b (c s) -> p b c s", s=width),
                                                       AX.X), f"mx{part}")
                    dve.wait_ge(dve_done.sem, dve_done.done(L, f"mx{part}"))
                    dve.wait_ge(act_done.sem, act_done.done(L, "negcq"))
                    nq = neg_cq[:, tile, first:first + n]
                    dve_done.sign(nc.vector.tensor_tensor(mxc[:, part, 0:n], mx[:, part, 0:n], nq, ALU.subtract), f"mxc{part}")
                    dve.wait_ge(dve_done.sem, dve_done.done(L, f"mxc{part}"))
                    dve_done.sign(nc.vector.scalar_tensor_tensor(out=bias[:, part, 0:n], in0=mxc[:, part, 0:n], scalar=-1.0,
                                                                 in1=nq, op0=ALU.mult, op1=ALU.subtract), f"bias{part}")

                def normalised(L, part):
                    n = 8 if part == 0 else 4
                    pr = p0 if part == 0 else p1[:, 4 * (part - 1):4 * part, :]
                    dve.wait_ge(act_done.sem, act_done.done(L, f"e{part}"))
                    dve_done.sign(nc.vector.reciprocal(pinv[:, part, 0:n], psums[:, part, 0:n]), f"inv{part}")
                    dve.wait_ge(dve_done.sem, dve_done.done(L, f"inv{part}"))
                    iv = pinv[:, part, 0:n].rearrange("p (h s) -> p h s", s=1).to_broadcast([P, n, pr.shape[-1]])
                    dve_done.sign(nc.vector.tensor_tensor(pr, pr, iv, ALU.mult), f"pn{part}")

                maxima(L, 0)
                lo(L, 45)
                dve.wait_ge(pool_done.sem, pool_done.done(L, ("rms", "sv")))
                for t in range(T):
                    dve_done.sign(nc.vector.scalar_tensor_tensor(
                        out=vb[:, t, :], in0=vb[:, t, :], scalar=rms[:, RMS["sv"], t:t + 1], in1=sgn[:, L, :],
                        op0=ALU.mult, op1=ALU.mult), ("vb", t))
                normalised(L, 0)
                lo(L, 46)
                maxima(L, 1)
                normalised(L, 1)
                lo(L, 47)
                maxima(L, 2)
                normalised(L, 2)
                lo(L, 48)
                lo(L, 49)
                lo(L, 50)
                for t in range(T):
                    result(L, "ah", t)
                    dve.wait_ge(act_done.sem, act_done.done(L, ("ac", t)))
                    dve_done.sign(nc.vector.scalar_tensor_tensor(
                        out=az[:, t, :], in0=ps[:, 2 * PAIR["ah"] + t, :], scalar=rms[:, RMS["mix"], t:t + 1],
                        in1=az[:, t, :], op0=ALU.mult, op1=ALU.mult), ("az", t))
                dve.wait_ge(mixed.sem, mixed.done(L, "pv"))
                dve_done.sign(nc.vector.memset(zp[:, :, 0:2], 0.0), "pad")
                lo(L, 51)
                dve.wait_ge(act_done.sem, act_done.done(L, "ychi"))
                dve_done.sign(nc.vector.tensor_tensor(y_lo[:, 0:4, :], ps[:, 4:6, :].rearrange("p b (c s) -> p (b c) s", c=2),
                                                      y_hi[:, 0:4, :].bitcast(F32), ALU.subtract), "yclo")
                lo(L, 52)
                dve.wait_ge(mixed.sem, mixed.done(L, "sg"))
                for t in range(T):
                    for g in range(GROUPS):
                        cols = slice(g * P, (g + 1) * P)
                        at = PAR["sgb"] + g
                        e = nc.vector.scalar_tensor_tensor(out=u[:, t, cols], in0=ps[:, 6 + t, cols], scalar=par[:, L, at:at + 1],
                                                           in1=u[:, t, cols], op0=ALU.add, op1=ALU.mult)
                    dve_done.sign(e, ("yb", t))
                lo(L, 53)
                dve.wait_ge(act_done.sem, act_done.done(L, "zp"))
                for i, shift in enumerate((2, 1, 0)):
                    for c in range(4):
                        at = PAR["conv"] + 4 * shift + c
                        tap = par[:, L, at:at + 1]
                        if i == 0:
                            e = nc.vector.tensor_scalar(ya[:, c, :], zp[:, c, 2:SEQ + 2], tap, None, ALU.mult)
                        else:
                            dve.wait_ge(conv_chain.sem, conv_chain.done(L, ("conv", i - 1, c)))
                            e = nc.vector.scalar_tensor_tensor(out=ya[:, c, :], in0=zp[:, c, shift:shift + SEQ], scalar=tap,
                                                               in1=ya[:, c, :], op0=ALU.mult, op1=ALU.add)
                        if i < 2:
                            conv_chain.sign(e, ("conv", i, c))
                dve_done.sign(e, "conv")
                lo(L, 54)
                dve.wait_ge(turned.sem, turned.done(L, "ab"))
                dve.wait_ge(dve_done.sem, dve_done.done(L, "conv"))
                dve_done.sign(nc.vector.tensor_tensor(ya, ps[:, 6:8, :].rearrange("p b (c s) -> p (b c) s", c=2), ya, ALU.mult), "ya")
                lo(L, 55)
                dve.wait_ge(act_done.sem, act_done.done(L, "ybhi"))
                dve_done.sign(nc.vector.tensor_tensor(y_lo[:, 4:8, :], ps[:, 4:6, :].rearrange("p b (c s) -> p (b c) s", c=2),
                                                      y_hi[:, 4:8, :].bitcast(F32), ALU.subtract), "yblo")
                lo(L, 56)
                dve.wait_ge(act_done.sem, act_done.done(L, "yahi"))
                dve_done.sign(nc.vector.tensor_tensor(y_lo[:, 8:12, :], ya, y_hi[:, 8:12, :].bitcast(F32), ALU.subtract), "yalo")
                for n in range(57, 66):
                    lo(L, n)

                slots_used = [0]

                def gate_branch(L, b):
                    half = int(b[1])
                    i = "abc".index(b[0])
                    for t in range(T):
                        result(L, b, t)
                        if t == 0:
                            dve.wait_ge(act_done.sem, act_done.done(L, ("g6", 1)))
                        at = i * D + half * W5
                        if b[0] == "c":
                            o = merged[:, t, half * W5:(half + 1) * W5]
                        else:
                            n = slots_used[0]
                            o = gated[:, n % 4, :]
                            if n >= 4:
                                dve.wait_ge(pool_done.sem, pool_done.done(L, ("add", "b" + b[1], t)))
                            slots_used[0] += 1
                        dve_done.sign(nc.vector.tensor_tensor(o, ps[:, 2 * PAIR[b] + t, :], gates[:, t, at:at + W5],
                                                              ALU.mult), (b, t))

                gate_branch(L, "c0")
                lo(L, 66)
                gate_branch(L, "c1")
                lo(L, 67)
                gate_branch(L, "b0")
                lo(L, 68)
                gate_branch(L, "b1")
                for t, h in TH1:
                    normed(L, "mem", t, h, y_lo)
                lo(L, 69)
                gate_branch(L, "a0")
                lo(L, 70)
                gate_branch(L, "a1")
                lo(L, 71)
                for t, h in TH1:
                    dve.wait_ge(act_done.sem, act_done.done(L, ("hi", "mg", t, h)))
                    cut = (slice(None), slice(4 * h, 4 * h + 4), slice(t * P, (t + 1) * P))
                    dve_done.sign(nc.vector.tensor_tensor(h_lo[cut], ps[:, 4 + 2 * t + h, :].rearrange("p (k s) -> p k s", k=4),
                                                          h_hi[cut].bitcast(F32), ALU.subtract), ("lo", "mg", t, h))
                for n in (72, 73, 74, 75):
                    lo(L, n)
                for t in range(T):
                    add_block(L, "wo0", "wo", t, 0)
                lo(L, 76)
                lo(L, 77)
                for t in range(T):
                    normed(L, "xa", t, 0, h_lo)
                for t in range(T):
                    add_block(L, "wo1", "wo", t, 1)
                lo(L, 78)
                for t in range(T):
                    normed(L, "xa", t, 1, h_lo)
                for n in (79, 80, 81, 82, 83):
                    lo(L, n)

                def xmaxima(L, part):
                    ab_ = "ab"[part]
                    dve.wait_ge(mixed.sem, mixed.done(L, "xs" + ab_))
                    dve_done.sign(nc.vector.reduce_max(xmx[:, part, :], ps[:, 4:6, :].rearrange("p b (c s) -> p (b c) s", c=2),
                                                       AX.X), "xmx" + ab_)
                    dve.wait_ge(dve_done.sem, dve_done.done(L, "xmx" + ab_))
                    dve_done.sign(nc.vector.tensor_scalar(xbias[:, part, :], xmx[:, part, :], -1.0, None, ALU.mult),
                                  "xbias" + ab_)

                def xnormalised(L, part):
                    ab_ = "ab"[part]
                    dve.wait_ge(act_done.sem, act_done.done(L, "xe" + ab_))
                    dve_done.sign(nc.vector.reciprocal(xinv[:, part, :], xsums[:, part, :]), "xinv" + ab_)
                    dve.wait_ge(dve_done.sem, dve_done.done(L, "xinv" + ab_))
                    pr = xp[part].rearrange("p t (h s) -> p (t h) s", h=2)
                    iv = xinv[:, part, :].rearrange("p (h s) -> p h s", s=1).to_broadcast([P, 4, SEQ])
                    dve_done.sign(nc.vector.tensor_tensor(pr, pr, iv, ALU.mult), "xpn" + ab_)

                xmaxima(L, 0)
                xnormalised(L, 0)
                lo(L, 84)
                lo(L, 85)
                xmaxima(L, 1)
                xnormalised(L, 1)
                lo(L, 86)
                lo(L, 87)
                for half, bank in ((0, 6), (1, 4)):
                    dve.wait_ge(act_done.sem, act_done.done(L, ("oahi", "obhi")[half]))
                    cut = (slice(None), slice(4 * half, 4 * half + 4), slice(0, SEQ))
                    dve_done.sign(nc.vector.tensor_tensor(h_lo[cut], ps[:, bank:bank + 2, :].rearrange("p b (c s) -> p (b c) s", c=2),
                                                          h_hi[cut].bitcast(F32), ALU.subtract), ("oalo", "oblo")[half])
                lo(L, 88)
                lo(L, 89)
                for t in range(T):
                    add_block(L, "xo0", "xo", t, 0)
                lo(L, 90)
                for t in range(T):
                    normed(L, "ffn2", t, 0, h_lo)
                lo(L, 91)
                for t in range(T):
                    add_block(L, "xo1", "xo", t, 1)
                for t in range(T):
                    normed(L, "ffn2", t, 1, h_lo)
                lo(L, 92)
                ffn(L, 2)
                for t in range(T):
                    add_down(L, 2, t)
            dve.wait_ge(consts_loaded, 16 * (2 + 3 * LAYERS))
            dve.wait_ge(ended, 4)
            for t in range(T):
                nc.vector.scalar_tensor_tensor(out=hg_out[:, t, :], in0=x[:, t, :], scalar=rms[:, RMS["end"], t:t + 1],
                                               in1=final_gain, op0=ALU.mult, op1=ALU.mult).then_inc(ended, 1)

        @block.tensor
        def _(pe):
            def passes(bank, stat_hi, stat_lo, mov_hi, mov_lo, start, stop):
                nc.tensor.matmul(bank, stat_hi, mov_hi, start=start, stop=False, skip_group_check=True)
                nc.tensor.matmul(bank, stat_hi, mov_lo, start=False, stop=False, skip_group_check=True)
                return nc.tensor.matmul(bank, stat_lo, mov_hi, start=False, stop=stop, skip_group_check=True)

            def unit(L, name, n, s_hi, s_lo, at0, tiles, bank0, width, first, last, acc, ready=None, free=None, more=0):
                s = n % SLOTS
                pe.wait_ge(lo_split.sem, lo_split.done(L, n, 3 * more))
                for t in range(T):
                    if free:
                        free(t)
                    if ready:
                        ready(t)
                    for j, kk in enumerate(tiles):
                        m = passes(ps[:, bank0 + t, 0:width], s_hi[:, at0 + kk, t * P:(t + 1) * P],
                                   s_lo[:, at0 + kk, t * P:(t + 1) * P], w_hi[:, s, j * W5:j * W5 + width],
                                   w_lo[:, s, j * W5:j * W5 + width], first and j == 0, last and j == len(tiles) - 1)
                    if last and t == 0:
                        acc_done.sign(m, acc)
                unit_used.sign(m, n)

            def turn(L, src, name, stage, t, h):
                for j in range(4):
                    kk = 4 * h + j
                    m = nc.tensor.transpose(ps[:, 4 + 2 * t + h, j * P:(j + 1) * P], src[:, t, kk * P:(kk + 1) * P], ident[:, :])
                turned.sign(m, ("t", stage, t, h))

            def turn_pair(L, src, bank, name):
                for c in range(4):
                    for t in range(T):
                        m = nc.tensor.transpose(ps[:, bank + c // 2, (c % 2) * SEQ + t * P:(c % 2) * SEQ + (t + 1) * P],
                                                src[:, t, c * P:(c + 1) * P], ident[:, :])
                turned.sign(m, name)

            def ffn(L, f):
                base = FFN_BASE[f]
                stage = f"ffn{f}"

                def gate_up(c, half, more=0):
                    n = base + (half if c == 0 else 3 * c - 1 + half)

                    def free(t):
                        if half == 0 and c > 0:
                            pe.wait_ge(dve_done.sem, dve_done.done(L, ("mul", f, c - 1, t), 3 * more))

                    def ready(t):
                        if c == 0:
                            pe.wait_ge(dve_done.sem, dve_done.done(L, ("lo", stage, t, half)))

                    unit(L, "gu", n, h_hi, h_lo, 0, range(4 * half, 4 * half + 4), 0, W5, half == 0, half == 1,
                         gu(f, c), ready, free, more)

                def turn_glu(c, more=0):
                    pe.wait_ge(dve_done.sem, dve_done.done(L, ("mul", f, c, 1), 3 * more))
                    if c > 0:
                        pe.wait_ge(dve_done.sem, dve_done.done(L, ("glulo", f, c - 1), 3 * more))
                    for j in range(2):
                        for t in range(T):
                            m = nc.tensor.transpose(ps[:, 2, j * SEQ + t * P:j * SEQ + (t + 1) * P],
                                                    glu[:, t, j * P:(j + 1) * P], ident[:, :])
                    turned.sign(m, ("glu", f, c))

                def down(c, more=0):
                    n = base + (FFN_UNITS - 1 if c == STEPS - 1 else 3 * c + 4)
                    s = n % SLOTS
                    last = c == STEPS - 1
                    pe.wait_ge(lo_split.sem, lo_split.done(L, n, 3 * more))
                    pe.wait_ge(dve_done.sem, dve_done.done(L, ("glulo", f, c), 3 * more))
                    for t in range(T):
                        for j in range(2):
                            for h in range(2):
                                at = j * D + h * W5
                                m = passes(ps[:, 4 + 2 * t + h, :], glu_hi[:, j, t * P:(t + 1) * P], glu_lo[:, j, t * P:(t + 1) * P],
                                           w_hi[:, s, at:at + W5], w_lo[:, s, at:at + W5], c == 0 and j == 0, last and j == 1)
                        if last and t == 0:
                            acc_done.sign(m, ("down", f))
                    unit_used.sign(m, n)

                def step(c, more=0):
                    gate_up(c, 0, more)
                    turn_glu(c - 1, more)
                    gate_up(c, 1, more)
                    down(c - 1, more)

                gate_up(0, 0)
                gate_up(0, 1)
                step(1)
                with pe.Fori(0, STEPS - 2) as more:
                    step(2, more)
                for s_, per in ((unit_used, 3), (acc_done, 1), (turned, 1)):
                    s_.skip(per * (STEPS - 3))
                turn_glu(STEPS - 1)
                down(STEPS - 1)

            def after(L, steps, name):
                pe.wait_ge(steps.sem, steps.done(L, name))

            FREE = {}
            for n in ("fg", "q", "k", "v", "sv", "su", "ac", "ab", "g1", "g2", "g3", "g4", "g5", "g6",
                      "xk0", "xk1", "xq0", "xq1", "xv0", "xv1"):
                FREE[n] = lambda t, n=n: (act_done, (n, t))
            FREE["ah"] = lambda t: (dve_done, ("az", t))
            for n in ("c0", "c1", "b0", "b1", "a0", "a1"):
                FREE[n] = lambda t, n=n: (dve_done, (n, t))
            for n, w, h in (("wo0", "wo", 0), ("wo1", "wo", 1), ("xo0", "xo", 0), ("xo1", "xo", 1)):
                FREE[n] = lambda t, w=w, h=h: (dve_done, ("x", w, t, h))
            TILES = dict(BLOCKS)

            def run_unit(L, name, i, s_hi, s_lo, at0=0, ready=None):
                tiles = TILES[name][i]
                width = GATE if name == "fg" or name[0] == "g" else W5

                def free(t):
                    if i == 0 and name in BEFORE:
                        after(L, *FREE[BEFORE[name]](t))

                unit(L, name, FIRST[name] + i, s_hi, s_lo, at0, tiles, 2 * PAIR[name], width, i == 0,
                     i == len(TILES[name]) - 1, name, ready, free)

            def run(L, name, s_hi, s_lo):
                run_unit(L, name, 0, s_hi, s_lo)
                run_unit(L, name, 1, s_hi, s_lo)

            pe.wait_ge(consts_made, 11 + LAYERS)
            pe.wait_ge(inputs_loaded, 16)
            with pe.Fori(0, LAYERS) as L:
                for t, h in TH1:
                    turn(L, x, "x", "ffn1", t, h)
                ffn(L, 1)
                for t in range(T):
                    for h in range(2):
                        after(L, dve_done, ("x", "f1", t, h))
                        turn(L, x, "x", "mix", t, h)
                for i in range(2):
                    run_unit(L, "fg", i, h_hi, h_lo, ready=lambda t, i=i: after(L, dve_done, ("lo", "mix", t, i)))
                run(L, "q", h_hi, h_lo)
                after(L, dve_done, "logf")
                after(L, dve_done, ("lo", "mix", 1, 1))
                lfs = lf[:, 3, :, :]
                nc.tensor.matmul(ps[0:HEADS, 7, 0:SEQ], lfs[:, 0, :], neg_upper[:, :], start=True, stop=False, skip_group_check=True)
                nc.tensor.matmul(ps[0:HEADS, 7, P:SEQ], lfs[:, 1, :], neg_upper[:, 0:P], start=False, stop=True, skip_group_check=True)
                nc.tensor.matmul(ps[:, 7, SEQ:SEQ + 8], neg_upper[:, 0:P], lfs[:, 0, :], start=True, stop=True, skip_group_check=True)
                nc.tensor.matmul(ps[:, 7, SEQ + 8:SEQ + 16], neg_upper[:, P:SEQ], lfs[:, 0, :], start=True, stop=False, skip_group_check=True)
                mixed.sign(nc.tensor.matmul(ps[:, 7, SEQ + 8:SEQ + 16], neg_upper[:, 0:P], lfs[:, 1, :], start=False, stop=True,
                                            skip_group_check=True), "c")
                run(L, "k", h_hi, h_lo)
                after(L, act_done, ("q", 1))
                turn_pair(L, q, 4, "q")
                run(L, "v", h_hi, h_lo)
                after(L, act_done, ("k", 1))
                after(L, act_done, "negcq")
                turn_pair(L, k, 6, "k")
                run(L, "sv", h_hi, h_lo)

                def scores(L, part):
                    bank, width, first, n, tile = {0: (4, P, 0, 8, 0), 1: (6, SEQ, 0, 4, 1), 2: (4, SEQ, 4, 4, 1)}[part]
                    for i in range(n):
                        h = first + i
                        rows = slice(HD * (h % 2), HD * (h % 2) + HD)
                        o = ps[:, bank + i % 2, i // 2 * width:(i // 2 + 1) * width]
                        nc.tensor.matmul(o, qt[rows, h // 2, tile * P:(tile + 1) * P], kt[rows, h // 2, 0:width],
                                         start=True, stop=False, skip_group_check=True)
                        nc.tensor.matmul(o, head_row[:, h, :], neg_c[:, 0:width], start=False, stop=False, skip_group_check=True)
                        m = nc.tensor.matmul(o[:, width - P:width], ident_bf[:, :], mask_bf[:, :], start=False, stop=True,
                                             skip_group_check=True)
                    mixed.sign(m, f"s{part}")

                after(L, act_done, "kt")
                scores(L, 0)
                run_unit(L, "su", 0, h_hi, h_lo)
                scores(L, 1)
                run_unit(L, "su", 1, h_hi, h_lo)
                run_unit(L, "ac", 0, h_hi, h_lo)
                after(L, act_done, "e0")
                scores(L, 2)
                run_unit(L, "ac", 1, h_hi, h_lo)

                after(L, dve_done, "pn1")
                for h in range(4):
                    nc.tensor.transpose(ps[:, 6 + h // 2, (h % 2) * SEQ:(h % 2) * SEQ + P], p0[:, h, :], ident[:, :])
                    m = nc.tensor.transpose(ps[:, 6 + h // 2, (h % 2) * SEQ + P:(h % 2) * SEQ + SEQ], p1[:, h, 0:P], ident[:, :])
                turned.sign(m, "p0")
                run_unit(L, "ah", 0, h_hi, h_lo)
                after(L, dve_done, "pn2")
                for h in range(4, 8):
                    nc.tensor.transpose(ps[:, 2 + h // 2, (h % 2) * SEQ:(h % 2) * SEQ + P], p0[:, h, :], ident[:, :])
                    m = nc.tensor.transpose(ps[:, 2 + h // 2, (h % 2) * SEQ + P:(h % 2) * SEQ + SEQ], p1[:, h, 0:P], ident[:, :])
                turned.sign(m, "p1")
                run_unit(L, "ah", 1, h_hi, h_lo)
                after(L, act_done, "pt0")
                for h in range(8):
                    m = nc.tensor.transpose(ps[:, 6 + h // 4, (h % 4) * P:(h % 4 + 1) * P], p1[:, h, P:SEQ], ident[:, :])
                turned.sign(m, "p2")
                run_unit(L, "ab", 0, h_hi, h_lo)
                after(L, act_done, "pt2")
                for h in range(HEADS):
                    rows = slice(HD * (h % 2), HD * (h % 2) + HD)
                    at = (h // 2 % 2) * SEQ
                    nc.tensor.matmul(ps[rows, 4 + h // 4, at:at + SEQ], v[:, 0, h * HD:(h + 1) * HD], pt0[:, h, :],
                                     start=True, stop=False, skip_group_check=True)
                    m = nc.tensor.matmul(ps[rows, 4 + h // 4, at + P:at + SEQ], v[:, 1, h * HD:(h + 1) * HD], pt1[:, h, :],
                                         start=False, stop=True, skip_group_check=True)
                mixed.sign(m, "pv")
                run_unit(L, "ab", 1, h_hi, h_lo)
                after(L, dve_done, ("vb", 1))
                after(L, pool_done, "sgw")
                for t in range(T):
                    for g in range(GROUPS):
                        m = nc.tensor.matmul(ps[:, 6 + t, g * P:(g + 1) * P], sgw[:, g * P:(g + 1) * P], vb[:, t, g * P:(g + 1) * P],
                                             start=True, stop=True, skip_group_check=True)
                mixed.sign(m, "sg")
                run_unit(L, "g1", 0, h_hi, h_lo)
                after(L, dve_done, "yclo")
                after(L, dve_done, ("az", 1))
                turn_pair(L, az, 4, "z")
                run_unit(L, "g1", 1, h_hi, h_lo)
                after(L, dve_done, ("yb", 1))
                after(L, act_done, ("ab", 1))
                turn_pair(L, ab, 6, "ab")
                run_unit(L, "g2", 0, h_hi, h_lo)
                after(L, act_done, "zp")
                turn_pair(L, u, 4, "yb")
                run_unit(L, "g2", 1, h_hi, h_lo)
                for n in ("g3", "g4", "g5", "g6"):
                    run(L, n, h_hi, h_lo)
                after(L, dve_done, "yalo")
                for b, at0 in (("c", 0), ("b", 4)):
                    for i in range(2):
                        run_unit(L, f"{b}{i}", 0, y_hi, y_lo, at0)
                pe.wait_ge(mem_loaded, L * 16 + 16)
                for t, h in TH1:
                    turn(L, mem, "mem", "mem", t, h)
                run_unit(L, "a0", 0, y_hi, y_lo, 8)
                run_unit(L, "a1", 0, y_hi, y_lo, 8)
                after(L, dve_done, ("lo", "mem", 1, 1))
                run_unit(L, "xk0", 0, y_hi, y_lo)
                after(L, pool_done, ("add", "a1", 1))
                for t, h in TH1:
                    turn(L, merged, "mg", "mg", t, h)
                run_unit(L, "xk0", 1, y_hi, y_lo)
                after(L, dve_done, ("lo", "mg", 1, 1))
                run_unit(L, "wo0", 0, h_hi, h_lo)
                run_unit(L, "wo0", 1, h_hi, h_lo)
                after(L, act_done, ("xk0", 1))
                turn_pair(L, xk, 4, "xk0")
                run_unit(L, "wo0", 2, h_hi, h_lo)
                run(L, "wo1", h_hi, h_lo)
                after(L, act_done, "xkt0")
                for t in range(T):
                    after(L, dve_done, ("x", "wo", t, 0))
                    turn(L, x, "x", "xa", t, 0)
                run_unit(L, "xk1", 0, y_hi, y_lo)
                for t in range(T):
                    after(L, dve_done, ("x", "wo", t, 1))
                    turn(L, x, "x", "xa", t, 1)
                run_unit(L, "xk1", 1, y_hi, y_lo)
                for i in range(2):
                    run_unit(L, "xq0", i, h_hi, h_lo, ready=lambda t, i=i: after(L, dve_done, ("lo", "xa", t, i)))
                after(L, act_done, ("xk1", 1))
                turn_pair(L, xk, 4, "xk1")
                run_unit(L, "xq1", 0, h_hi, h_lo)
                after(L, act_done, ("xq0", 1))
                turn_pair(L, xq[0], 6, "xq0")
                run_unit(L, "xq1", 1, h_hi, h_lo)

                def xscores(L, part):
                    for t in range(T):
                        for j in range(2):
                            for c in range(2):
                                kk = 4 * part + 2 * j + c
                                m = nc.tensor.matmul(ps[:, 4 + t, j * SEQ:(j + 1) * SEQ], xqt[:, kk, t * P:(t + 1) * P], xkt[:, kk, :],
                                                     start=c == 0, stop=c == 1, skip_group_check=True)
                    mixed.sign(m, "xs" + "ab"[part])

                after(L, act_done, "xqt0")
                xscores(L, 0)
                run_unit(L, "xv0", 0, y_hi, y_lo)
                after(L, act_done, ("xq1", 1))
                turn_pair(L, xq[1], 6, "xq1")
                run_unit(L, "xv0", 1, y_hi, y_lo)
                after(L, act_done, "xqt1")
                xscores(L, 1)

                def xturn(L, part, bank):
                    after(L, dve_done, "xpn" + "ab"[part])
                    for h in range(2):
                        for kk in range(2):
                            for t in range(T):
                                m = nc.tensor.transpose(ps[:, bank + h, kk * SEQ + t * P:kk * SEQ + (t + 1) * P],
                                                        xp[part][:, t, h * SEQ + kk * P:h * SEQ + (kk + 1) * P], ident[:, :])
                    turned.sign(m, "xp" + "ab"[part])

                run_unit(L, "xv1", 0, y_hi, y_lo)
                xturn(L, 0, 6)
                run_unit(L, "xv1", 1, y_hi, y_lo)
                xturn(L, 1, 4)

                def xvalues(L, part, bank):
                    for h in range(2):
                        for c in range(2):
                            for kk in range(2):
                                at = (2 * part + h) * SEQ + c * P
                                m = nc.tensor.matmul(ps[:, bank + h, c * SEQ:(c + 1) * SEQ], xv[:, kk, at:at + P],
                                                     xpt[:, 2 * part + h, kk, :], start=kk == 0, stop=kk == 1, skip_group_check=True)
                    mixed.sign(m, "xv" + "ab"[part])

                after(L, act_done, "xpt0")
                xvalues(L, 0, 6)
                after(L, act_done, "xpt1")
                xvalues(L, 1, 4)
                after(L, dve_done, "oalo")
                run_unit(L, "xo0", 0, h_hi, h_lo)
                after(L, dve_done, "oblo")
                run_unit(L, "xo0", 1, h_hi, h_lo)
                run_unit(L, "xo1", 0, h_hi, h_lo)
                for t in range(T):
                    after(L, dve_done, ("x", "xo", t, 0))
                    turn(L, x, "x", "ffn2", t, 0)
                run_unit(L, "xo1", 1, h_hi, h_lo)
                for t in range(T):
                    after(L, dve_done, ("x", "xo", t, 1))
                    turn(L, x, "x", "ffn2", t, 1)
                ffn(L, 2)
                after(L, dve_done, ("x", "f2", 1, 1))


_INS = ["weights", "x", "mem", "params", "sg_norm", "sg_w", "fox_b_f", "final_norm"]


def _layout(i):
    import numpy as np

    def tiles(w, rows, cols):
        u = np.zeros((P, UNIT), w.dtype)
        for j, r in enumerate(rows):
            part = w[r * P:(r + 1) * P, cols]
            u[:, j * W5:j * W5 + part.shape[1]] = part
        return u

    units = []
    w_in_cols = {}
    names = ["ab", "ac", "ah", "su", "sv", "q", "k", "v"]
    for n, name in enumerate(names):
        w_in_cols[name] = slice(n * W5, (n + 1) * W5)
    for n, name in enumerate(["fg", "g1", "g2", "g3", "g4", "g5", "g6"]):
        w_in_cols[name] = slice(8 * W5 + n * GATE, 8 * W5 + (n + 1) * GATE)

    def ffn_units(l, f):
        g, up, dn = (np.asarray(i[f"ffn{f}_w_{n}"][l]) for n in ("gate", "up", "down"))

        def gate_up(c, half):
            u = np.empty((P, 4, 2, FC), g.dtype)
            for j in range(4):
                r = slice((4 * half + j) * P, (4 * half + j + 1) * P)
                u[:, j, 0] = g[r, c * FC:(c + 1) * FC]
                u[:, j, 1] = up[r, c * FC:(c + 1) * FC]
            return u.reshape(P, UNIT)

        def down(c):
            return dn[c * FC:(c + 1) * FC].reshape(2, P, D).transpose(1, 0, 2).reshape(P, UNIT)

        out = [gate_up(0, 0), gate_up(0, 1)]
        for c in range(1, STEPS):
            out += [gate_up(c, 0), gate_up(c, 1), down(c - 1)]
        return out + [down(STEPS - 1)]

    for l in range(LAYERS):
        units += ffn_units(l, 1)
        for name, parts in BLOCKS:
            half = slice(int(name[-1]) * W5, (int(name[-1]) + 1) * W5) if name[-1].isdigit() else None
            if name in w_in_cols:
                w, cols = np.asarray(i["w_in"][l]), w_in_cols[name]
            elif name[0] in "abc":
                w, cols = np.asarray(i["w_branch"][l]["abc".index(name[0])]), half
            elif name[:2] == "wo":
                w, cols = np.asarray(i["w_out"][l]), half
            else:
                w, cols = np.asarray(i["xa_w" + name[1]][l]), half
            units += [tiles(w, r, cols) for r in parts]
        units += ffn_units(l, 2)
    params = []
    for l in range(LAYERS):
        cols = [np.asarray(i[n][l]).reshape(KT, P).T for n in ("ffn1_norm", "mix_norm", "mem_norm", "xa_norm", "ffn2_norm")]
        cols.append(np.asarray(i["conv_w"][l]).reshape(3 * 4, P).T)
        cols.append(np.asarray(i["sg_b"][l]).T)
        params.append(np.concatenate(cols, axis=1))
    return {
        "weights": np.stack(units),
        "x": np.asarray(i["x"]).reshape(SEQ, D),
        "mem": np.asarray(i["mem"]).reshape(SEQ, D),
        "params": np.stack(params),
        "sg_norm": np.asarray(i["sg_norm"]),
        "sg_w": np.asarray(i["sg_w"]).transpose(0, 3, 1, 2).reshape(LAYERS, P, GROUPS * P),
        "fox_b_f": np.asarray(i["fox_b_f"]),
        "final_norm": np.asarray(i["final_norm"]).reshape(1, D),
    }


def kernel(**inputs):
    import numpy as _np
    import concourse.bacc as _bacc
    from concourse.bass_utils import run_bass_kernel_spmd as _run

    nc = _bacc.Bacc("TRN2", target_bir_lowering=False, num_devices=1)
    laid = _layout(inputs)
    arrays, args = {}, []
    for name in _INS:
        a = _np.ascontiguousarray(laid[name])
        arrays[f"in_{name}"] = a
        args.append(nc.dram_tensor(f"in_{name}", a.shape, mybir.dt.from_np(a.dtype), kind="ExternalInput").ap())
    out = nc.dram_tensor("out_0", (SEQ, D), F32, kind="ExternalOutput").ap()
    trunk(nc, *args, out)
    r = _run(nc, [arrays], core_ids=[0])
    return r.results[0]["out_0"].reshape(1, SEQ, D)
```

```python
import concourse.bass as bass
from concourse import mybir
from concourse.alu_op_type import AluOpType as ALU
from contextlib import ExitStack

F32 = mybir.dt.float32
F32R = mybir.dt.float32r
BF16 = mybir.dt.bfloat16
ACT = mybir.ActivationFunctionType
AX = mybir.AxisListType

LAYERS = 2
P = 128
T = 2
SEQ = T * P
D = 1024
KT = D // P
FF = 2816
FC = 256
STEPS = FF // FC
TURN = 2
assert (STEPS - 3) % TURN == 0 and TURN % 2 == 0
W5 = 512
UNIT = 2048
SLOTS = 3
HEADS, HD = 8, 64
XH = 4
GROUPS = 4
EPS = 1e-6
GATE = 440
FFN_UNITS = 3 * STEPS
NEG = -1e30

BLOCKS = [(n, [range(0, 4), range(4, 8)]) for n in
          ("fg", "q", "k", "v", "sv", "su", "ac", "ah", "ab", "g1", "g2", "g3", "g4", "g5", "g6")]
BLOCKS += [(n, [range(0, 4)]) for n in ("c0", "c1", "b0", "b1", "a0", "a1")]
BLOCKS += [("xk0", [range(0, 4), range(4, 8)]),
           ("wo0", [range(0, 3), range(3, 6), range(6, 8)]), ("wo1", [range(0, 4), range(4, 8)])]
BLOCKS += [(n, [range(0, 4), range(4, 8)]) for n in ("xk1", "xq0", "xq1", "xv0", "xv1", "xo0", "xo1")]
FIRST = {}
LAST = {}
_u = FFN_UNITS
for _n, _k in BLOCKS:
    FIRST[_n], LAST[_n] = _u, _u + len(_k) - 1
    _u += len(_k)
FFN_BASE = {1: 0, 2: _u}
UNITS = _u + FFN_UNITS
assert UNITS % SLOTS == 0 and FFN_BASE[2] % SLOTS == 0 and FFN_UNITS % SLOTS == 0
PAIR = {n: (i + 1) % 2 for i, (n, _) in enumerate(BLOCKS)}
BEFORE = {n: BLOCKS[i - 2][0] for i, (n, _) in enumerate(BLOCKS) if i >= 2}

NPAR = 5 * KT + 12 + GROUPS
PAR = {"ffn1": 0, "mix": 8, "mem": 16, "xa": 24, "ffn2": 32, "conv": 40, "sgb": 52}
RMS = {"ffn1": 0, "mix": 1, "sv": 2, "mem": 3, "xa": 4, "ffn2": 5, "end": 6}


class Steps:

    def __init__(self, sem, names, start=0):
        self.sem, self.names, self.start = sem, names, start
        self.at_name = {n: i + 1 for i, n in enumerate(names)}
        assert len(self.at_name) == len(names)
        self.next = 0

    def done(self, layer, name, more=0):
        return layer * len(self.names) + (self.start + self.at_name[name] + more)

    def done_before(self, layer, last=0):
        return layer * len(self.names) + (self.start - last)

    def sign(self, instruction, name):
        assert self.names[self.next % len(self.names)] == name, (self.names[self.next % len(self.names)], name)
        self.next += 1
        return instruction.then_inc(self.sem, 1)

    def skip(self, n):
        self.next += n


def trunk(nc, weights, x_in, mem_in, params, sg_norm, sg_w, fox_b, final_g, out):
    ctx = ExitStack()
    with ctx:
        def sb(name, shape, dt=F32):
            return ctx.enter_context(nc.sbuf_tensor(name, shape, dt))

        def sem(name):
            return ctx.enter_context(nc.semaphore(name))

        raw = sb("raw", [P, SLOTS, UNIT])
        w_hi = sb("w_hi", [P, SLOTS, UNIT], F32R)
        w_lo = sb("w_lo", [P, SLOTS, UNIT], F32R)
        x = sb("x", [P, T, D])
        hg = sb("hg", [P, 2, W5])
        h_hi = sb("h_hi", [P, KT, SEQ], F32R)
        h_lo = sb("h_lo", [P, KT, SEQ], F32R)
        y_hi = sb("y_hi", [P, 12, SEQ], F32R)
        y_lo = sb("y_lo", [P, 12, SEQ], F32R)
        r1 = sb("r1", [P, 6144])
        r2 = sb("r2", [P, 7184])
        fg = sb("fg", [P, T, GATE])
        par = sb("par", [P, LAYERS, NPAR])
        sgn = sb("sgn", [P, LAYERS, W5])
        sgw_all = sb("sgw_all", [P, LAYERS, W5])
        sgw = sb("sgw", [P, W5])
        foxb = sb("foxb", [P, LAYERS, HEADS])
        warm = sb("warm", [P, 1])
        junk = sb("junk", [P, D], BF16)
        ident = sb("ident", [P, P])
        ident_bf = sb("ident_bf", [P, P], BF16)
        mask_bf = sb("mask_bf", [P, P], BF16)
        head_row = sb("head_row", [P, HEADS, P], F32R)
        neg_upper = sb("neg_upper", [P, SEQ])
        squares = sb("squares", [P, 7, T])
        eps = sb("eps", [P, T])
        meansq = sb("meansq", [P, 7, T])
        rms = sb("rms", [P, 7, T])
        half_power = sb("half_power", [P, T])
        lf = sb("lf", [P, 3, T, HEADS])
        log_f = sb("log_f", [P, T, P])
        neg_c = sb("neg_c", [P, SEQ], F32R)
        neg_cq = sb("neg_cq", [P, T, HEADS])
        mx = sb("mx", [P, 3, HEADS])
        mxc = sb("mxc", [P, 3, HEADS])
        bias = sb("bias", [P, 3, HEADS])
        psums = sb("psums", [P, 3, HEADS])
        pinv = sb("pinv", [P, 3, HEADS])
        xmx = sb("xmx", [P, 2, 4])
        xbias = sb("xbias", [P, 2, 4])
        xsums = sb("xsums", [P, 2, 4])
        xinv = sb("xinv", [P, 2, 4])
        ps = ctx.enter_context(nc.psum_tensor("ps", [P, 8, W5], F32))

        def view(t, at, *shape):
            n = 1
            for s in shape:
                n *= s
            v = t[:, at:at + n]
            if len(shape) == 1:
                return v
            if len(shape) == 2:
                return v.rearrange("p (a b) -> p a b", b=shape[1])
            return v.rearrange("p (a b c) -> p a b c", b=shape[1], c=shape[2])

        silu = view(r1, 0, T, FC)
        glu = view(r1, 512, T, FC)
        glu_hi = [y_hi[:, 2 * i:2 * i + 2, :] for i in range(2)]
        glu_lo = [y_lo[:, 2 * i:2 * i + 2, :] for i in range(2)]
        p0 = view(r1, 0, HEADS, P)
        p1 = view(r1, 1024, HEADS, SEQ)
        pt0 = view(r1, 3072, HEADS, SEQ)
        pt1 = view(r1, 5120, HEADS, P)
        gates = view(r1, 0, T, 3 * D)
        q, k, v = view(r2, 0, T, W5), view(r2, 1024, T, W5), view(r2, 2048, T, W5)
        qt, kt = view(r2, 3072, 4, SEQ), view(r2, 4096, 4, SEQ)
        u, vb = view(r2, 5120, T, W5), view(r2, 6144, T, W5)
        az, ab = view(r2, 0, T, W5), view(r2, 1024, T, W5)
        zp = view(r2, 2048, 4, SEQ + 2)
        ya = view(r2, 4096, 4, SEQ)
        merged = view(r2, 5120, T, D)
        gated = view(r2, 0, 4, W5)
        mem = view(r2, 2048, T, D)
        m_hi, m_lo = y_hi[:, 0:KT, :], y_lo[:, 0:KT, :]
        xkt, xqt, xv = view(r1, 0, KT, SEQ), view(r1, 2048, KT, SEQ), view(r1, 4096, T, D)
        xk = view(r2, 0, T, W5)
        xq = [view(r2, 1024, T, W5), view(r2, 2048, T, W5)]
        xp = [view(r2, 3072, T, W5), view(r2, 4096, T, W5)]
        xpt = view(r2, 5120, XH, T, SEQ)

        heads_made = view(r2, 0, HEADS, P)
        hg_out = view(r1, 0, T, D)
        final_gain = view(r1, 2048, D)

        raw_loaded = [sem(f"raw_loaded{i}") for i in range(SLOTS)]
        x_loaded = [sem(f"x_loaded{t}") for t in range(T)]
        params_loaded = sem("params_loaded")
        consts_loaded = sem("consts_loaded")
        mem_loaded = sem("mem_loaded")
        ident_made = sem("ident_made")
        consts_made = sem("consts_made")
        CONSTS = 12 + LAYERS
        hi_split = Steps(sem("hi_split"), list(range(UNITS)))
        lo_split = Steps(sem("lo_split"), list(range(UNITS)))
        unit_used = Steps(sem("unit_used"), list(range(UNITS)), start=SLOTS)
        out_stored = sem("out_stored")
        last_squares = sem("last_squares")
        last_mean = sem("last_mean")
        last_rms = sem("last_rms")
        gain_loaded = sem("gain_loaded")
        out_made = sem("out_made")

        TH1 = [(0, 0), (0, 1), (1, 0), (1, 1)]
        TH2 = [(0, 0), (1, 0), (0, 1), (1, 1)]

        def th(kind, stage):
            return [(kind, stage, t, h) for t, h in TH2]

        def gu(f, c):
            return ("gu", f, c)

        acc_done = Steps(sem("acc_done"),
                         [gu(1, c) for c in range(STEPS)] + [("down", 1)] + [n for n, _ in BLOCKS]
                         + [gu(2, c) for c in range(STEPS)] + [("down", 2)])
        turned = Steps(sem("turned"),
                       th("t", "ffn1") + [("glu", 1, c) for c in range(STEPS)] + th("t", "mix")
                       + ["q", "k", "p0", "p1", "p2", "z", "ab", "yb"] + th("t", "mem") + th("t", "mg")
                       + ["xk0"] + th("t", "xa") + ["xk1", "xq0", "xq1", "xpa", "xpb"]
                       + th("t", "ffn2") + [("glu", 2, c) for c in range(STEPS)])
        mixed = Steps(sem("mixed"), ["c", "s0", "s1", "s2", "pv", "sg", "xsa", "xsb", "xva", "xvb"])

        def act_ffn(f):
            return [("silu", f, 0, 0), ("silu", f, 0, 1)] + \
                [s for c in range(1, STEPS) for s in (("gluhi", f, c - 1), ("silu", f, c, 0), ("silu", f, c, 1))] + \
                [("gluhi", f, STEPS - 1)]

        def sq(stage):
            return [("sq", stage, 0), ("sq", stage, 1)]

        act_done = Steps(sem("act_done"),
                         th("hi", "ffn1") + sq("ffn1") + act_ffn(1) + th("hi", "mix") + sq("mix")
                         + [("fg", 0), ("fg", 1), "exp", "ln", ("q", 0), ("q", 1), "negc", "negcq",
                            ("k", 0), ("k", 1), "qt", ("v", 0), ("v", 1), "kt",
                            "e0", ("sv", 0), ("sv", 1)] + sq("sv")
                         + [("su", 0), ("su", 1), "e1", "e2", ("ac", 0), ("ac", 1), "pt0", "pt1", "pt2",
                            "ychi", ("ab", 0), ("ab", 1), "zp", ("g0", 0), ("g0", 1), ("g1", 0), ("g1", 1),
                            "ybhi", ("g2", 0), ("g2", 1), "yahi"]
                         + [(g, t) for g in ("g3", "g4", "g5", "g6") for t in range(T)]
                         + sq("mem") + th("hi", "mem") + th("hi", "mg") + [("xk0", 0), ("xk0", 1), "xkt0"]
                         + th("hi", "xa") + sq("xa") + [("xk1", 0), ("xk1", 1), ("xq0", 0), ("xq0", 1), "xkt1", "xqt0",
                            ("xq1", 0), ("xq1", 1), "xea", "xqt1", ("xv0", 0), ("xv0", 1), "xeb", "xpt0",
                            ("xv1", 0), ("xv1", 1), "xpt1", "oahi", "obhi"]
                         + th("hi", "ffn2") + sq("ffn2") + act_ffn(2))

        def dve_ffn(f):
            return [("mul", f, 0, 0), ("mul", f, 0, 1)] + \
                [s for c in range(1, STEPS) for s in (("glulo", f, c - 1), ("mul", f, c, 0), ("mul", f, c, 1))] + \
                [("glulo", f, STEPS - 1)]

        def xn(stage, order):
            return [("x", stage, t, h) for t, h in order]

        def norm_dve(stage, h):
            return [(step, stage, t, h) for step in ("hg", "lo") for t in range(T)]

        dve_done = Steps(sem("dve_done"),
                         [(step, "ffn1", t, 0) for t in range(T) for step in ("hg", "lo")] + norm_dve("ffn1", 1) + dve_ffn(1)
                         + xn("f1", TH1[0:3]) + norm_dve("mix", 0)[0:3] + xn("f1", TH1[3:4]) + norm_dve("mix", 0)[3:4]
                         + norm_dve("mix", 1)
                         + ["z", "az", "logf", "neglo", "mx0", "mxc0", "bias0", ("vb", 0), ("vb", 1), "inv0", "pn0",
                            "mx1", "mxc1", "bias1", "inv1", "pn1", "mx2", "mxc2", "bias2", "inv2", "pn2",
                            ("az", 0), ("az", 1), "pad", "yclo", ("yb", 0), ("yb", 1), "conv", "ya", "yblo", "yalo"]
                         + [(b, t) for b in ("c0", "c1") for t in range(T)] + norm_dve("mem", 0)
                         + [(b, t) for b in ("b0", "b1") for t in range(T)] + norm_dve("mem", 1)
                         + [(b, t) for b in ("a0", "a1") for t in range(T)]
                         + th("lo", "mg") + xn("wo", [(0, 0), (1, 0)])
                         + norm_dve("xa", 0) + xn("wo", [(0, 1), (1, 1)])
                         + norm_dve("xa", 1)
                         + ["xmxa", "xbiasa", "xinva", "xpna", "xmxb", "xbiasb", "xinvb", "xpnb", "oalo", "oblo"]
                         + xn("xo", [(0, 0), (1, 0)]) + norm_dve("ffn2", 0)
                         + xn("xo", [(0, 1), (1, 1)]) + norm_dve("ffn2", 1)
                         + dve_ffn(2) + xn("f2", TH1),
                         start=4)
        conv_chain = Steps(sem("conv_chain"), [("conv", i, c) for i in range(2) for c in range(4)])
        pool_done = Steps(sem("pool_done"),
                          ["sgw"] + [(m, s) for s in ("ffn1", "mix", "sv", "mem") for m in ("mean", "rms")]
                          + [("add", b, t) for b in ("b0", "b1", "a0", "a1") for t in range(T)]
                          + [(m, s) for s in ("xa", "ffn2") for m in ("mean", "rms")])

        block = ctx.enter_context(nc.Block())

        @block.sync
        def _(sp):
            for s in range(SLOTS):
                if s < T:
                    sp.dma_start(x[:, s, :], x_in[s * P:(s + 1) * P, :]).then_inc(x_loaded[s], 16)
                sp.dma_start(raw[:, s, :], weights[s, :, :]).then_inc(raw_loaded[s], 16)
            with sp.Fori(1, LAYERS * UNITS // SLOTS) as turn:
                for s in range(SLOTS):
                    sp.wait_ge(lo_split.sem, (turn - 1) * SLOTS + (s + 1))
                    sp.dma_start(raw[:, s, :], weights[turn * SLOTS + s, :, :]).then_inc(raw_loaded[s], 16)
            for n, (t, h) in enumerate(TH1):
                sp.wait_ge(out_made, n + 1)
                cols = slice(h * W5, (h + 1) * W5)
                sp.dma_start(out[t * P:(t + 1) * P, cols], hg_out[:, t, cols]).then_inc(out_stored, 16)
            sp.wait_ge(out_stored, 16 * len(TH1))

        @block.gpsimd
        def _(pool):
            pool.dma_start(par[:, :, :], params.rearrange("l p n -> p l n")).then_inc(params_loaded, 16)
            nc.gpsimd.memset(ident[:, :], 0.0).then_inc(ident_made, 1)
            pool.wait_ge(ident_made, 1)
            nc.gpsimd.affine_select(out=ident[:, :], in_=ident[:, :], compare_op=ALU.not_equal, fill=1.0, base=0,
                                    pattern=[[-1, P]], channel_multiplier=1).then_inc(ident_made, 1)
            for l in range(LAYERS):
                pool.dma_start(sgn[:, l, :], sg_norm[l:l + 1, :].to_broadcast([P, W5])).then_inc(consts_loaded, 16)
                pool.dma_start(foxb[:, l, :], fox_b[l:l + 1, :].to_broadcast([P, HEADS])).then_inc(consts_loaded, 16)
                pool.dma_start(sgw_all[:, l, :], sg_w[l, :, :]).then_inc(consts_loaded, 16)
            nc.gpsimd.memset(half_power[:, :], -0.5).then_inc(consts_made, 1)
            nc.gpsimd.memset(eps[:, :], EPS).then_inc(consts_made, 1)
            nc.gpsimd.memset(mask_bf[:, :], 0.0).then_inc(consts_made, 1)
            nc.gpsimd.memset(heads_made, 0.0).then_inc(consts_made, 1)
            nc.gpsimd.memset(log_f[:, :, :], 0.0).then_inc(consts_made, 1)
            nc.gpsimd.memset(neg_upper[:, :], -1.0).then_inc(consts_made, 1)
            pool.wait_ge(consts_made, 6)
            nc.gpsimd.affine_select(out=mask_bf[:, :], in_=mask_bf[:, :], compare_op=ALU.is_ge, fill=NEG, base=0,
                                    pattern=[[-1, P]], channel_multiplier=1).then_inc(consts_made, 1)
            for n, row in enumerate((0, 32)):
                pool.wait_ge(consts_made, 7 + n)
                nc.gpsimd.affine_select(out=heads_made, in_=heads_made, compare_op=ALU.not_equal, fill=1.0,
                                        base=-row, pattern=[[-1, HEADS], [0, P]], channel_multiplier=1).then_inc(consts_made, 1)
            pool.wait_ge(consts_made, 9)
            nc.gpsimd.tensor_copy(head_row[:, :, :], heads_made).then_inc(consts_made, 1)
            nc.gpsimd.affine_select(out=neg_upper[:, 0:P], in_=neg_upper[:, 0:P], compare_op=ALU.is_ge, fill=0.0,
                                    base=0, pattern=[[1, P]], channel_multiplier=-1).then_inc(consts_made, 1)
            pool.wait_ge(ident_made, 2)
            nc.gpsimd.tensor_copy(ident_bf[:, :], ident[:, :]).then_inc(consts_made, 1)
            pool.wait_ge(consts_loaded, 16 * 3 * LAYERS)
            for l in range(LAYERS):
                sw = sgw_all[:, l, :].rearrange("p (g t) -> p g t", g=GROUPS)
                nc.gpsimd.affine_select(out=sw, in_=sw, compare_op=ALU.is_ge, fill=0.0, base=0,
                                        pattern=[[0, GROUPS], [1, P]], channel_multiplier=-1).then_inc(consts_made, 1)

            def inverse_rms(L, stage, last_square):
                i = RMS[stage]
                pool.wait_ge(act_done.sem, last_square)
                m = nc.gpsimd.tensor_tensor(meansq[:, i, :], squares[:, i, :], eps[:, :], ALU.add)
                pool_done.sign(m, ("mean", stage))
                pool.wait_ge(pool_done.sem, pool_done.done(L, ("mean", stage)))
                r = nc.gpsimd.tensor_tensor(rms[:, i, :], meansq[:, i, :], half_power[:, :], ALU.pow)
                pool_done.sign(r, ("rms", stage))

            pool.wait_ge(consts_made, CONSTS)
            with pool.Fori(0, LAYERS) as L:
                pool_done.sign(nc.gpsimd.tensor_copy(sgw[:, :], sgw_all[:, L, :]), "sgw")
                for stage in ("ffn1", "mix", "sv"):
                    inverse_rms(L, stage, act_done.done(L, ("sq", stage, 1)))
                inverse_rms(L, "mem", act_done.done(L, ("sq", "mem", 1)))
                slot = 0
                for b in ("b0", "b1", "a0", "a1"):
                    half = int(b[1])
                    for t in range(T):
                        pool.wait_ge(dve_done.sem, dve_done.done(L, (b, t)))
                        if b[0] == "a":
                            pool.wait_ge(pool_done.sem, pool_done.done(L, ("add", "b" + b[1], t)))
                        m = merged[:, t, half * W5:(half + 1) * W5]
                        pool_done.sign(nc.gpsimd.tensor_tensor(m, m, gated[:, slot % 4, :], ALU.add), ("add", b, t))
                        slot += 1
                inverse_rms(L, "xa", act_done.done(L, ("sq", "xa", 1)))
                inverse_rms(L, "ffn2", act_done.done(L, ("sq", "ffn2", 1)))
            pool.dma_start(final_gain, final_g.to_broadcast([P, D])).then_inc(gain_loaded, 16)
            i = RMS["end"]
            for t in range(T):
                pool.wait_ge(last_squares, t + 1)
                nc.gpsimd.tensor_tensor(meansq[:, i, t:t + 1], squares[:, i, t:t + 1], eps[:, 0:1], ALU.add).then_inc(last_mean, 1)
                pool.wait_ge(last_mean, t + 1)
                nc.gpsimd.tensor_tensor(rms[:, i, t:t + 1], meansq[:, i, t:t + 1], half_power[:, 0:1], ALU.pow).then_inc(last_rms, 1)

        @block.scalar
        def _(act):
            def hi(L, n):
                s = n % SLOTS
                act.wait_ge(raw_loaded[s], L * (16 * UNITS // SLOTS) + 16 * (n // SLOTS + 1))
                act.wait_ge(unit_used.sem, unit_used.done_before(L, SLOTS - (n + 1)))
                hi_split.sign(nc.scalar.copy(w_hi[:, s, :], raw[:, s, :]), n)

            def result(L, name, t):
                if t == 0:
                    act.wait_ge(acc_done.sem, acc_done.done(L, name))
                else:
                    act.wait_ge(unit_used.sem, unit_used.done(L, LAST[name]))

            def rms_ready(L, stage):
                act.wait_ge(pool_done.sem, pool_done.done(L, ("rms", stage)))

            def take(L, name, t, out_ap, stage, func=ACT.Copy, cols=slice(0, W5)):
                result(L, name, t)
                b = 2 * PAIR[name] + t
                act_done.sign(nc.scalar.activation(out_ap, ps[:, b, cols], func,
                                                   scale=rms[:, RMS[stage], t:t + 1]),
                              (name, t))

            def split_norm(L, stage, t, h, hi_ap):
                act.wait_ge(dve_done.sem, dve_done.done(L, ("hg", stage, t, h)))
                act_done.sign(nc.scalar.copy(hi_ap[:, 4 * h:4 * h + 4, t * P:(t + 1) * P],
                                             hg[:, t, :].rearrange("p (k s) -> p k s", k=4)), ("hi", stage, t, h))

            def square(L, stage, t, src, width):
                if t == 1:
                    if stage == "end":
                        act.wait_ge(last_squares, 1)
                    else:
                        act.wait_ge(act_done.sem, act_done.done(L, ("sq", stage, 0)))
                return nc.scalar.activation(junk[:, 0:width], src, ACT.Square,
                                            scale=width ** -0.5, accum_out=squares[:, RMS[stage], t:t + 1])

            def ffn(L, f):
                base = FFN_BASE[f]
                stage = f"ffn{f}"

                def silus(c, more_a=0, more_u=0):
                    for t in range(T):
                        if t == 0:
                            act.wait_ge(acc_done.sem, acc_done.done(L, gu(f, c), more_a))
                        else:
                            act.wait_ge(unit_used.sem, unit_used.done(L, base + (1 if c == 0 else 3 * c), more_u))
                        if c == 0 and t == 0:
                            rms_ready(L, stage)
                        if c > 0:
                            act.wait_ge(dve_done.sem, dve_done.done(L, ("mul", f, c - 1, t), 3 * more_a))
                        act_done.sign(nc.scalar.activation(silu[:, t, :], ps[:, t, 0:FC], ACT.Silu,
                                                           scale=rms[:, RMS[stage], t:t + 1]), ("silu", f, c, t))

                def glu_split(c, more=0):
                    act.wait_ge(turned.sem, turned.done(L, ("glu", f, c), more))
                    if c > 1:
                        act.wait_ge(unit_used.sem, unit_used.done(L, base + 3 * c - 2, 3 * more))
                    act_done.sign(nc.scalar.copy(glu_hi[c % 2], ps[:, 2, :].rearrange("p (k s) -> p k s", k=2)), ("gluhi", f, c))

                def step(c, more=0):
                    for i in range(3):
                        if i == 1:
                            glu_split(c - 1, more)
                        n = base + 3 * c + i
                        act.wait_ge(raw_loaded[i], L * (16 * UNITS // SLOTS) + (16 * ((base + 3 * c) // SLOTS + 1) + 16 * more))
                        act.wait_ge(unit_used.sem, unit_used.done(L, n - SLOTS, 3 * more))
                        hi_split.sign(nc.scalar.copy(w_hi[:, i, :], raw[:, i, :]), n)
                    silus(c, more, 3 * more)

                silus(0)
                step(1)
                with act.Fori(0, STEPS - 3, TURN) as more:
                    for i in range(TURN):
                        step(2 + i, more)
                hi_split.skip(3 * (STEPS - 3 - TURN))
                act_done.skip(3 * (STEPS - 3 - TURN))
                step(STEPS - 1)
                if f == 1:
                    hi(L, FFN_UNITS)
                glu_split(STEPS - 1)

            act.wait_ge(ident_made, 2)
            with act.Fori(0, LAYERS) as L:

                def splits(stage, h, hi_ap=h_hi):
                    for t in range(T):
                        split_norm(L, stage, t, h, hi_ap)

                nc.scalar.copy(warm[:, :], ident[:, 0:1])
                hi(L, 0)
                splits("ffn1", 0)
                hi(L, 1)
                splits("ffn1", 1)
                hi(L, 2)
                for t in range(T):
                    act_done.sign(square(L, "ffn1", t, x[:, t, :], D), ("sq", "ffn1", t))
                ffn(L, 1)
                hi(L, 34)
                splits("mix", 0)
                splits("mix", 1)
                hi(L, 35)
                for t in range(T):
                    act_done.sign(square(L, "mix", t, x[:, t, :], D), ("sq", "mix", t))
                hi(L, 36)
                rms_ready(L, "mix")
                for t in range(T):
                    take(L, "fg", t, fg[:, t, :], "mix", cols=slice(0, GATE))
                hi(L, 37)
                act.wait_ge(dve_done.sem, dve_done.done(L, "az"))
                act_done.sign(nc.scalar.activation(lf[:, 1, :, :], lf[:, 1, :, :], ACT.Exp, scale=-1.0), "exp")
                act.wait_ge(act_done.sem, act_done.done(L, "exp"))
                act_done.sign(nc.scalar.activation(lf[:, 2, :, :], lf[:, 1, :, :], ACT.Ln, bias=1.0), "ln")
                hi(L, 38)
                for t in range(T):
                    take(L, "q", t, q[:, t, :], "mix")
                act.wait_ge(mixed.sem, mixed.done(L, "c"))
                act_done.sign(nc.scalar.copy(neg_c[:, :], ps[:, 7, 0:SEQ]), "negc")
                act_done.sign(nc.scalar.copy(neg_cq[:, :, :], ps[:, 7, SEQ:SEQ + 16].rearrange("p (t h) -> p t h", t=T)), "negcq")
                hi(L, 39)
                hi(L, 40)
                for t in range(T):
                    take(L, "k", t, k[:, t, :], "mix")
                act.wait_ge(turned.sem, turned.done(L, "q"))
                act_done.sign(nc.scalar.mul(qt, ps[:, 4:6, :].rearrange("p b (c s) -> p (b c) s", c=2), HD ** -0.5), "qt")
                hi(L, 41)
                hi(L, 42)
                for t in range(T):
                    take(L, "v", t, v[:, t, :], "mix")
                act.wait_ge(turned.sem, turned.done(L, "k"))
                act_done.sign(nc.scalar.copy(kt, ps[:, 6:8, :].rearrange("p b (c s) -> p (b c) s", c=2)), "kt")
                hi(L, 43)
                hi(L, 44)

                def exps(L, part, n, name):
                    act.wait_ge(dve_done.sem, dve_done.done(L, f"bias{part}"))
                    bank, width = {0: (4, P), 1: (6, SEQ), 2: (4, SEQ)}[part]
                    for i in range(n):
                        h = i + (4 if part == 2 else 0)
                        o = p0[:, h, :] if part == 0 else p1[:, h, :]
                        e = nc.scalar.activation(o, ps[:, bank + i % 2, i // 2 * width:(i // 2 + 1) * width], ACT.Exp,
                                                 bias=bias[:, part, i:i + 1], accum_out=psums[:, part, i:i + 1])
                    act_done.sign(e, name)

                exps(L, 0, HEADS, "e0")
                hi(L, 45)
                for t in range(T):
                    take(L, "sv", t, vb[:, t, :], "mix", ACT.Gelu_apprx_tanh)
                for t in range(T):
                    act.wait_ge(act_done.sem, act_done.done(L, ("sv", t)))
                    act_done.sign(square(L, "sv", t, vb[:, t, :], W5), ("sq", "sv", t))
                hi(L, 46)
                for t in range(T):
                    take(L, "su", t, u[:, t, :], "mix", ACT.Gelu_apprx_tanh)
                exps(L, 1, 4, "e1")
                hi(L, 47)
                exps(L, 2, 4, "e2")
                hi(L, 48)
                for t in range(T):
                    take(L, "ac", t, az[:, t, :], "mix")

                def probs_out(L, name, where, bank):
                    act.wait_ge(turned.sem, turned.done(L, name))
                    act_done.sign(nc.scalar.copy(where, ps[:, bank:bank + 2, :].rearrange(
                        "p b (c s) -> p (b c) s", s=where.shape[-1])), {"p0": "pt0", "p1": "pt1", "p2": "pt2"}[name])

                probs_out(L, "p0", pt0[:, 0:4, :], 6)
                hi(L, 49)
                probs_out(L, "p1", pt0[:, 4:8, :], 4)
                hi(L, 50)
                probs_out(L, "p2", pt1, 6)
                hi(L, 51)
                act.wait_ge(mixed.sem, mixed.done(L, "pv"))
                act_done.sign(nc.scalar.copy(y_hi[:, 0:4, :], ps[:, 4:6, :].rearrange("p b (c s) -> p (b c) s", c=2)), "ychi")
                hi(L, 52)
                for t in range(T):
                    take(L, "ab", t, ab[:, t, :], "mix")
                hi(L, 53)
                act.wait_ge(turned.sem, turned.done(L, "z"))
                act_done.sign(nc.scalar.copy(zp[:, :, 2:SEQ + 2], ps[:, 4:6, :].rearrange("p b (c s) -> p (b c) s", c=2)), "zp")
                for t in range(T):
                    act_done.sign(nc.scalar.activation(gates[:, t, 0:GATE - HEADS], fg[:, t, HEADS:GATE], ACT.Sigmoid),
                                  ("g0", t))
                hi(L, 54)

                def gate(L, i):
                    at = GATE * i - HEADS
                    for t in range(T):
                        take(L, f"g{i}", t, gates[:, t, at:at + GATE], "mix", ACT.Sigmoid, cols=slice(0, GATE))

                gate(L, 1)
                hi(L, 55)
                act.wait_ge(turned.sem, turned.done(L, "yb"))
                act_done.sign(nc.scalar.copy(y_hi[:, 4:8, :], ps[:, 4:6, :].rearrange("p b (c s) -> p (b c) s", c=2)), "ybhi")
                hi(L, 56)
                gate(L, 2)
                act.wait_ge(dve_done.sem, dve_done.done(L, "ya"))
                act.dma_start(mem, mem_in.rearrange("(t p) d -> p t d", p=P)).then_inc(mem_loaded, 16)
                act_done.sign(nc.scalar.copy(y_hi[:, 8:12, :], ya), "yahi")
                hi(L, 57)
                hi(L, 58)
                for i in (3, 4, 5, 6):
                    gate(L, i)
                    hi(L, 59 + 2 * (i - 3))
                    if i < 6:
                        hi(L, 60 + 2 * (i - 3))
                act.wait_ge(mem_loaded, L * 16 + 16)
                for t in range(T):
                    act_done.sign(square(L, "mem", t, mem[:, t, :], D), ("sq", "mem", t))
                hi(L, 66)
                hi(L, 67)
                splits("mem", 0, m_hi)
                hi(L, 68)
                hi(L, 69)
                splits("mem", 1, m_hi)
                hi(L, 70)
                hi(L, 71)
                for t, h in TH2:
                    act.wait_ge(turned.sem, turned.done(L, ("t", "mg", t, h)))
                    act_done.sign(nc.scalar.copy(h_hi[:, 4 * h:4 * h + 4, t * P:(t + 1) * P],
                                                 ps[:, 4 + 2 * t + h, :].rearrange("p (k s) -> p k s", k=4)),
                                  ("hi", "mg", t, h))
                hi(L, 72)
                rms_ready(L, "mem")
                for t in range(T):
                    take(L, "xk0", t, xk[:, t, :], "mem")
                hi(L, 73)
                hi(L, 74)

                def turned_out(L, name, what, where, bank, scale=1.0):
                    act.wait_ge(turned.sem, turned.done(L, name))
                    act_done.sign(nc.scalar.mul(where, ps[:, bank:bank + 2, :].rearrange("p b (c s) -> p (b c) s", c=2), scale), what)

                turned_out(L, "xk0", "xkt0", xkt[:, 0:4, :], 4)
                hi(L, 75)
                hi(L, 76)
                hi(L, 77)
                splits("xa", 0)
                hi(L, 78)
                splits("xa", 1)
                hi(L, 79)
                for t in range(T):
                    act_done.sign(square(L, "xa", t, x[:, t, :], D), ("sq", "xa", t))
                for t in range(T):
                    take(L, "xk1", t, xk[:, t, :], "mem")
                hi(L, 80)
                hi(L, 81)
                rms_ready(L, "xa")
                for t in range(T):
                    take(L, "xq0", t, xq[0][:, t, :], "xa")
                turned_out(L, "xk1", "xkt1", xkt[:, 4:8, :], 4)
                hi(L, 82)
                turned_out(L, "xq0", "xqt0", xqt[:, 0:4, :], 6, (D // XH) ** -0.5)
                hi(L, 83)
                for t in range(T):
                    take(L, "xq1", t, xq[1][:, t, :], "xa")

                def xexps(L, part, name):
                    act.wait_ge(dve_done.sem, dve_done.done(L, "xbias" + "ab"[part]))
                    for i in range(4):
                        t, h = i // 2, i % 2
                        e = nc.scalar.activation(xp[part][:, t, h * SEQ:(h + 1) * SEQ],
                                                 ps[:, 4 + t, h * SEQ:(h + 1) * SEQ], ACT.Exp,
                                                 bias=xbias[:, part, i:i + 1], accum_out=xsums[:, part, i:i + 1])
                    act_done.sign(e, name)

                xexps(L, 0, "xea")
                hi(L, 84)
                turned_out(L, "xq1", "xqt1", xqt[:, 4:8, :], 6, (D // XH) ** -0.5)
                hi(L, 85)
                for t in range(T):
                    take(L, "xv0", t, xv[:, t, 0:W5], "mem")
                xexps(L, 1, "xeb")
                hi(L, 86)
                act.wait_ge(turned.sem, turned.done(L, "xpa"))
                act_done.sign(nc.scalar.copy(xpt[:, 0:2, :, :].rearrange("p h k s -> p (h k s)"),
                                             ps[:, 6:8, :].rearrange("p b s -> p (b s)")), "xpt0")
                hi(L, 87)
                for t in range(T):
                    take(L, "xv1", t, xv[:, t, W5:D], "mem")
                act.wait_ge(turned.sem, turned.done(L, "xpb"))
                act_done.sign(nc.scalar.copy(xpt[:, 2:4, :, :].rearrange("p h k s -> p (h k s)"),
                                             ps[:, 4:6, :].rearrange("p b s -> p (b s)")), "xpt1")
                for half, (m, bank) in enumerate((("xva", 6), ("xvb", 4))):
                    act.wait_ge(mixed.sem, mixed.done(L, m))
                    act_done.sign(nc.scalar.copy(h_hi[:, 4 * half:4 * half + 4, :],
                                                 ps[:, bank:bank + 2, :].rearrange("p b (c s) -> p (b c) s", c=2)),
                                  ("oahi", "obhi")[half])
                hi(L, 88)
                hi(L, 89)
                hi(L, 90)
                splits("ffn2", 0)
                hi(L, 91)
                splits("ffn2", 1)
                hi(L, 92)
                for t in range(T):
                    act_done.sign(square(L, "ffn2", t, x[:, t, :], D), ("sq", "ffn2", t))
                ffn(L, 2)
            for t in range(T):
                act.wait_ge(dve_done.sem, dve_done.done_before(LAYERS, 2 * (T - 1 - t)))
                square(0, "end", t, x[:, t, :], D).then_inc(last_squares, 1)

        @block.vector
        def _(dve):
            def lo_of(n, s):
                return lo_split.sign(nc.vector.tensor_tensor(w_lo[:, s, :], raw[:, s, :], w_hi[:, s, :].bitcast(F32),
                                                             ALU.subtract), n)

            def lo(L, n):
                dve.wait_ge(hi_split.sem, hi_split.done(L, n))
                lo_of(n, n % SLOTS)

            def result(L, name, t):
                if t == 0:
                    dve.wait_ge(acc_done.sem, acc_done.done(L, name))
                else:
                    dve.wait_ge(unit_used.sem, unit_used.done(L, LAST[name]))

            def gain(L, stage):
                at = PAR[stage]
                return par[:, L, at:at + KT]

            hg_tiles = hg[:, :, :].rearrange("p t (k s) -> p t k s", k=4)

            def gained(L, stage, t, h):
                at = PAR[stage] + 4 * h
                dve.wait_ge(turned.sem, turned.done(L, ("t", stage, t, h)))
                if h == 1:
                    dve.wait_ge(dve_done.sem, dve_done.done(L, ("lo", stage, t, 0)))
                g = par[:, L, at:at + 4].rearrange("p (k s) -> p k s", s=1).to_broadcast([P, 4, P])
                dve_done.sign(nc.vector.tensor_tensor(hg_tiles[:, t], ps[:, 4 + 2 * t + h, :].rearrange("p (k s) -> p k s", k=4),
                                                      g, ALU.mult), ("hg", stage, t, h))

            def lo_half(L, stage, t, h, hi_ap=h_hi, lo_ap=h_lo):
                dve.wait_ge(act_done.sem, act_done.done(L, ("hi", stage, t, h)))
                cut = (slice(None), slice(4 * h, 4 * h + 4), slice(t * P, (t + 1) * P))
                dve_done.sign(nc.vector.tensor_tensor(lo_ap[cut], hg_tiles[:, t], hi_ap[cut].bitcast(F32), ALU.subtract),
                              ("lo", stage, t, h))

            def normed(L, stage, h, between=None, **where):
                for t in range(T):
                    gained(L, stage, t, h)
                lo_half(L, stage, 0, h, **where)
                if between:
                    between()
                lo_half(L, stage, 1, h, **where)

            def add_down(L, f, t, h):
                if t == 0:
                    dve.wait_ge(acc_done.sem, acc_done.done(L, ("down", f)))
                else:
                    dve.wait_ge(unit_used.sem, unit_used.done(L, FFN_BASE[f] + FFN_UNITS - 1))
                xs = x[:, t, h * W5:(h + 1) * W5]
                dve_done.sign(nc.vector.scalar_tensor_tensor(out=xs, in0=ps[:, 4 + 2 * t + h, :], scalar=0.5, in1=xs,
                                                             op0=ALU.mult, op1=ALU.add), ("x", f"f{f}", t, h))

            def add_block(L, name, what, t, h):
                result(L, name, t)
                xs = x[:, t, h * W5:(h + 1) * W5]
                dve_done.sign(nc.vector.tensor_tensor(xs, ps[:, 2 * PAIR[name] + t, :], xs, ALU.add), ("x", what, t, h))

            def ffn(L, f):
                base = FFN_BASE[f]
                i_rms = RMS[f"ffn{f}"]

                def muls(c, more=0):
                    for t in range(T):
                        dve.wait_ge(act_done.sem, act_done.done(L, ("silu", f, c, t), 3 * more))
                        if c > 0:
                            dve.wait_ge(turned.sem, turned.done(L, ("glu", f, c - 1), more))
                        dve_done.sign(nc.vector.scalar_tensor_tensor(
                            out=glu[:, t, :], in0=ps[:, t, FC:2 * FC], scalar=rms[:, i_rms, t:t + 1], in1=silu[:, t, :],
                            op0=ALU.mult, op1=ALU.mult), ("mul", f, c, t))

                def glu_split(c, more=0):
                    dve.wait_ge(act_done.sem, act_done.done(L, ("gluhi", f, c), 3 * more))
                    dve_done.sign(nc.vector.tensor_tensor(glu_lo[c % 2], ps[:, 2, :].rearrange("p (k s) -> p k s", k=2),
                                                          glu_hi[c % 2].bitcast(F32), ALU.subtract), ("glulo", f, c))

                def step(c, more=0):
                    for i in range(3):
                        if i == 1:
                            glu_split(c - 1, more)
                        n = base + 3 * c + i
                        dve.wait_ge(hi_split.sem, hi_split.done(L, n, 3 * more))
                        lo_of(n, i)
                    muls(c, more)

                muls(0)
                step(1)
                with dve.Fori(0, STEPS - 3, TURN) as more:
                    for i in range(TURN):
                        step(2 + i, more)
                lo_split.skip(3 * (STEPS - 3 - TURN))
                dve_done.skip(3 * (STEPS - 3 - TURN))
                step(STEPS - 1)
                glu_split(STEPS - 1)

            dve.sem_inc(dve_done.sem, dve_done.start)
            dve.wait_ge(params_loaded, 16)
            with dve.Fori(0, LAYERS) as L:
                gained(L, "ffn1", 0, 0)
                lo(L, 0)
                lo_half(L, "ffn1", 0, 0)
                gained(L, "ffn1", 1, 0)
                lo_half(L, "ffn1", 1, 0)
                lo(L, 1)
                normed(L, "ffn1", 1)
                lo(L, 2)
                ffn(L, 1)
                lo(L, 33)
                for t, h in TH1[0:3]:
                    add_down(L, 1, t, h)
                normed(L, "mix", 0, between=lambda: add_down(L, 1, 1, 1))
                lo(L, 34)
                normed(L, "mix", 1)
                lo(L, 35)
                lo(L, 36)
                dve.wait_ge(act_done.sem, act_done.done(L, ("fg", 1)))
                dve.wait_ge(consts_loaded, 16 * 3 * LAYERS)
                dve_done.sign(nc.vector.tensor_tensor(lf[:, 0, :, :], fg[:, :, 0:HEADS],
                                                      foxb[:, L, :].rearrange("p (a h) -> p a h", a=1).to_broadcast([P, T, HEADS]),
                                                      ALU.add), "z")
                dve.wait_ge(dve_done.sem, dve_done.done(L, "z"))
                dve_done.sign(nc.vector.scalar_tensor_tensor(out=lf[:, 1, :, :], in0=lf[:, 0, :, :], scalar=-1.0,
                                                             in1=lf[:, 0, :, :], op0=ALU.mult, op1=ALU.max), "az")
                lo(L, 37)
                dve.wait_ge(act_done.sem, act_done.done(L, "ln"))
                dve.wait_ge(consts_made, CONSTS)
                for at in (0, 32):
                    e = nc.vector.scalar_tensor_tensor(out=log_f[:, :, at:at + HEADS], in0=lf[:, 0, :, :], scalar=0.0,
                                                       in1=lf[:, 2, :, :], op0=ALU.min, op1=ALU.subtract)
                dve_done.sign(e, "logf")
                for n in range(38, 45):
                    lo(L, n)
                    if n == 40:
                        dve.wait_ge(act_done.sem, act_done.done(L, "negc"))
                        dve_done.sign(nc.vector.tensor_tensor(neg_c[32:64, :], ps[32:64, 7, 0:SEQ],
                                                              neg_c[32:64, :].bitcast(F32), ALU.subtract), "neglo")

                def maxima(L, part):
                    dve.wait_ge(mixed.sem, mixed.done(L, f"s{part}"))
                    bank, width, n = {0: (4, P, 8), 1: (6, SEQ, 4), 2: (4, SEQ, 4)}[part]
                    tile, first = (0, 0) if part == 0 else (1, 0 if part == 1 else 4)
                    dve_done.sign(nc.vector.reduce_max(mx[:, part, 0:n].rearrange("p (c b) -> p b c", b=2),
                                                       ps[:, bank:bank + 2, :].rearrange("p b (c s) -> p b c s", s=width),
                                                       AX.X), f"mx{part}")
                    dve.wait_ge(dve_done.sem, dve_done.done(L, f"mx{part}"))
                    dve.wait_ge(act_done.sem, act_done.done(L, "negcq"))
                    nq = neg_cq[:, tile, first:first + n]
                    dve_done.sign(nc.vector.tensor_tensor(mxc[:, part, 0:n], mx[:, part, 0:n], nq, ALU.subtract), f"mxc{part}")
                    dve.wait_ge(dve_done.sem, dve_done.done(L, f"mxc{part}"))
                    dve_done.sign(nc.vector.scalar_tensor_tensor(out=bias[:, part, 0:n], in0=mxc[:, part, 0:n], scalar=-1.0,
                                                                 in1=nq, op0=ALU.mult, op1=ALU.subtract), f"bias{part}")

                def normalised(L, part):
                    n = 8 if part == 0 else 4
                    pr = p0 if part == 0 else p1[:, 4 * (part - 1):4 * part, :]
                    dve.wait_ge(act_done.sem, act_done.done(L, f"e{part}"))
                    dve_done.sign(nc.vector.reciprocal(pinv[:, part, 0:n], psums[:, part, 0:n]), f"inv{part}")
                    dve.wait_ge(dve_done.sem, dve_done.done(L, f"inv{part}"))
                    iv = pinv[:, part, 0:n].rearrange("p (h s) -> p h s", s=1).to_broadcast([P, n, pr.shape[-1]])
                    dve_done.sign(nc.vector.tensor_tensor(pr, pr, iv, ALU.mult), f"pn{part}")

                maxima(L, 0)
                lo(L, 45)
                dve.wait_ge(pool_done.sem, pool_done.done(L, ("rms", "sv")))
                for t in range(T):
                    dve_done.sign(nc.vector.scalar_tensor_tensor(
                        out=vb[:, t, :], in0=vb[:, t, :], scalar=rms[:, RMS["sv"], t:t + 1], in1=sgn[:, L, :],
                        op0=ALU.mult, op1=ALU.mult), ("vb", t))
                normalised(L, 0)
                lo(L, 46)
                maxima(L, 1)
                normalised(L, 1)
                lo(L, 47)
                maxima(L, 2)
                normalised(L, 2)
                lo(L, 48)
                lo(L, 49)
                lo(L, 50)
                for t in range(T):
                    result(L, "ah", t)
                    dve.wait_ge(act_done.sem, act_done.done(L, ("ac", t)))
                    dve_done.sign(nc.vector.scalar_tensor_tensor(
                        out=az[:, t, :], in0=ps[:, 2 * PAIR["ah"] + t, :], scalar=rms[:, RMS["mix"], t:t + 1],
                        in1=az[:, t, :], op0=ALU.mult, op1=ALU.mult), ("az", t))
                dve.wait_ge(mixed.sem, mixed.done(L, "pv"))
                dve_done.sign(nc.vector.memset(zp[:, :, 0:2], 0.0), "pad")
                lo(L, 51)
                dve.wait_ge(act_done.sem, act_done.done(L, "ychi"))
                dve_done.sign(nc.vector.tensor_tensor(y_lo[:, 0:4, :], ps[:, 4:6, :].rearrange("p b (c s) -> p (b c) s", c=2),
                                                      y_hi[:, 0:4, :].bitcast(F32), ALU.subtract), "yclo")
                lo(L, 52)
                dve.wait_ge(mixed.sem, mixed.done(L, "sg"))
                for t in range(T):
                    for g in range(GROUPS):
                        cols = slice(g * P, (g + 1) * P)
                        at = PAR["sgb"] + g
                        e = nc.vector.scalar_tensor_tensor(out=u[:, t, cols], in0=ps[:, 6 + t, cols], scalar=par[:, L, at:at + 1],
                                                           in1=u[:, t, cols], op0=ALU.add, op1=ALU.mult)
                    dve_done.sign(e, ("yb", t))
                lo(L, 53)
                dve.wait_ge(act_done.sem, act_done.done(L, "zp"))
                for i, shift in enumerate((2, 1, 0)):
                    for c in range(4):
                        at = PAR["conv"] + 4 * shift + c
                        tap = par[:, L, at:at + 1]
                        if i == 0:
                            e = nc.vector.tensor_scalar(ya[:, c, :], zp[:, c, 2:SEQ + 2], tap, None, ALU.mult)
                        else:
                            dve.wait_ge(conv_chain.sem, conv_chain.done(L, ("conv", i - 1, c)))
                            e = nc.vector.scalar_tensor_tensor(out=ya[:, c, :], in0=zp[:, c, shift:shift + SEQ], scalar=tap,
                                                               in1=ya[:, c, :], op0=ALU.mult, op1=ALU.add)
                        if i < 2:
                            conv_chain.sign(e, ("conv", i, c))
                dve_done.sign(e, "conv")
                lo(L, 54)
                dve.wait_ge(turned.sem, turned.done(L, "ab"))
                dve.wait_ge(dve_done.sem, dve_done.done(L, "conv"))
                dve_done.sign(nc.vector.tensor_tensor(ya, ps[:, 6:8, :].rearrange("p b (c s) -> p (b c) s", c=2), ya, ALU.mult), "ya")
                lo(L, 55)
                dve.wait_ge(act_done.sem, act_done.done(L, "ybhi"))
                dve_done.sign(nc.vector.tensor_tensor(y_lo[:, 4:8, :], ps[:, 4:6, :].rearrange("p b (c s) -> p (b c) s", c=2),
                                                      y_hi[:, 4:8, :].bitcast(F32), ALU.subtract), "yblo")
                lo(L, 56)
                dve.wait_ge(act_done.sem, act_done.done(L, "yahi"))
                dve_done.sign(nc.vector.tensor_tensor(y_lo[:, 8:12, :], ya, y_hi[:, 8:12, :].bitcast(F32), ALU.subtract), "yalo")
                for n in range(57, 66):
                    lo(L, n)

                slots_used = [0]

                def gate_branch(L, b):
                    half = int(b[1])
                    i = "abc".index(b[0])
                    for t in range(T):
                        result(L, b, t)
                        if t == 0:
                            dve.wait_ge(act_done.sem, act_done.done(L, ("g6", 1)))
                        at = i * D + half * W5
                        if b[0] == "c":
                            o = merged[:, t, half * W5:(half + 1) * W5]
                        else:
                            n = slots_used[0]
                            o = gated[:, n % 4, :]
                            if n >= 4:
                                dve.wait_ge(pool_done.sem, pool_done.done(L, ("add", "b" + b[1], t)))
                            slots_used[0] += 1
                        dve_done.sign(nc.vector.tensor_tensor(o, ps[:, 2 * PAIR[b] + t, :], gates[:, t, at:at + W5],
                                                              ALU.mult), (b, t))

                gate_branch(L, "c0")
                lo(L, 66)
                gate_branch(L, "c1")
                lo(L, 67)
                normed(L, "mem", 0, hi_ap=y_hi, lo_ap=y_lo)
                lo(L, 68)
                gate_branch(L, "b0")
                gate_branch(L, "b1")
                lo(L, 69)
                normed(L, "mem", 1, hi_ap=y_hi, lo_ap=y_lo)
                gate_branch(L, "a0")
                lo(L, 70)
                gate_branch(L, "a1")
                lo(L, 71)
                for t, h in TH2:
                    dve.wait_ge(act_done.sem, act_done.done(L, ("hi", "mg", t, h)))
                    cut = (slice(None), slice(4 * h, 4 * h + 4), slice(t * P, (t + 1) * P))
                    dve_done.sign(nc.vector.tensor_tensor(h_lo[cut], ps[:, 4 + 2 * t + h, :].rearrange("p (k s) -> p k s", k=4),
                                                          h_hi[cut].bitcast(F32), ALU.subtract), ("lo", "mg", t, h))
                for n in (72, 73, 74, 75):
                    lo(L, n)
                for t in range(T):
                    add_block(L, "wo0", "wo", t, 0)
                lo(L, 76)
                lo(L, 77)
                normed(L, "xa", 0)
                for t in range(T):
                    add_block(L, "wo1", "wo", t, 1)
                lo(L, 78)
                normed(L, "xa", 1)
                for n in (79, 80, 81, 82, 83):
                    lo(L, n)

                def xmaxima(L, part):
                    ab_ = "ab"[part]
                    dve.wait_ge(mixed.sem, mixed.done(L, "xs" + ab_))
                    dve_done.sign(nc.vector.reduce_max(xmx[:, part, :], ps[:, 4:6, :].rearrange("p b (c s) -> p (b c) s", c=2),
                                                       AX.X), "xmx" + ab_)
                    dve.wait_ge(dve_done.sem, dve_done.done(L, "xmx" + ab_))
                    dve_done.sign(nc.vector.tensor_scalar(xbias[:, part, :], xmx[:, part, :], -1.0, None, ALU.mult),
                                  "xbias" + ab_)

                def xnormalised(L, part):
                    ab_ = "ab"[part]
                    dve.wait_ge(act_done.sem, act_done.done(L, "xe" + ab_))
                    dve_done.sign(nc.vector.reciprocal(xinv[:, part, :], xsums[:, part, :]), "xinv" + ab_)
                    dve.wait_ge(dve_done.sem, dve_done.done(L, "xinv" + ab_))
                    pr = xp[part].rearrange("p t (h s) -> p (t h) s", h=2)
                    iv = xinv[:, part, :].rearrange("p (h s) -> p h s", s=1).to_broadcast([P, 4, SEQ])
                    dve_done.sign(nc.vector.tensor_tensor(pr, pr, iv, ALU.mult), "xpn" + ab_)

                xmaxima(L, 0)
                xnormalised(L, 0)
                lo(L, 84)
                lo(L, 85)
                xmaxima(L, 1)
                xnormalised(L, 1)
                lo(L, 86)
                lo(L, 87)
                for half, bank in ((0, 6), (1, 4)):
                    dve.wait_ge(act_done.sem, act_done.done(L, ("oahi", "obhi")[half]))
                    cut = (slice(None), slice(4 * half, 4 * half + 4), slice(0, SEQ))
                    dve_done.sign(nc.vector.tensor_tensor(h_lo[cut], ps[:, bank:bank + 2, :].rearrange("p b (c s) -> p (b c) s", c=2),
                                                          h_hi[cut].bitcast(F32), ALU.subtract), ("oalo", "oblo")[half])
                lo(L, 88)
                lo(L, 89)
                for t in range(T):
                    add_block(L, "xo0", "xo", t, 0)
                lo(L, 90)
                normed(L, "ffn2", 0)
                for t in range(T):
                    add_block(L, "xo1", "xo", t, 1)
                lo(L, 91)
                normed(L, "ffn2", 1)
                lo(L, 92)
                ffn(L, 2)
                for t, h in TH1:
                    add_down(L, 2, t, h)
            dve.wait_ge(gain_loaded, 16)
            for t, h in TH1:
                cols = slice(h * W5, (h + 1) * W5)
                dve.wait_ge(last_rms, t + 1)
                nc.vector.scalar_tensor_tensor(out=hg_out[:, t, cols], in0=x[:, t, cols], scalar=rms[:, RMS["end"], t:t + 1],
                                               in1=final_gain[:, cols], op0=ALU.mult, op1=ALU.mult).then_inc(out_made, 1)

        @block.tensor
        def _(pe):
            def passes(bank, stat_hi, stat_lo, mov_hi, mov_lo, start, stop):
                nc.tensor.matmul(bank, stat_hi, mov_hi, start=start, stop=False, skip_group_check=True)
                nc.tensor.matmul(bank, stat_hi, mov_lo, start=False, stop=False, skip_group_check=True)
                return nc.tensor.matmul(bank, stat_lo, mov_hi, start=False, stop=stop, skip_group_check=True)

            def unit(L, name, n, s_hi, s_lo, at0, tiles, bank0, width, first, last, acc, ready=None, free=None, more=0):
                s = n % SLOTS
                pe.wait_ge(lo_split.sem, lo_split.done(L, n, 3 * more))
                for t in range(T):
                    if free:
                        free(t)
                    if ready:
                        ready(t)
                    for j, kk in enumerate(tiles):
                        m = passes(ps[:, bank0 + t, 0:width], s_hi[:, at0 + kk, t * P:(t + 1) * P],
                                   s_lo[:, at0 + kk, t * P:(t + 1) * P], w_hi[:, s, j * W5:j * W5 + width],
                                   w_lo[:, s, j * W5:j * W5 + width], first and j == 0, last and j == len(tiles) - 1)
                    if last and t == 0:
                        acc_done.sign(m, acc)
                unit_used.sign(m, n)

            def turn(L, src, name, stage, t, h):
                for j in range(4):
                    kk = 4 * h + j
                    m = nc.tensor.transpose(ps[:, 4 + 2 * t + h, j * P:(j + 1) * P], src[:, t, kk * P:(kk + 1) * P], ident[:, :])
                turned.sign(m, ("t", stage, t, h))

            def turn_pair(L, src, bank, name):
                for c in range(4):
                    for t in range(T):
                        m = nc.tensor.transpose(ps[:, bank + c // 2, (c % 2) * SEQ + t * P:(c % 2) * SEQ + (t + 1) * P],
                                                src[:, t, c * P:(c + 1) * P], ident[:, :])
                turned.sign(m, name)

            def ffn(L, f, inside_first=None):
                base = FFN_BASE[f]
                stage = f"ffn{f}"

                def gate_up(c, half, more=0, between=None):
                    n = base + (half if c == 0 else 3 * c - 1 + half)

                    def free(t):
                        if half == 0 and c > 0:
                            pe.wait_ge(dve_done.sem, dve_done.done(L, ("mul", f, c - 1, t), 3 * more))

                    def ready(t):
                        if between and t == 1:
                            between()
                        if c == 0:
                            pe.wait_ge(dve_done.sem, dve_done.done(L, ("lo", stage, t, half)))

                    unit(L, "gu", n, h_hi, h_lo, 0, range(4 * half, 4 * half + 4), 0, W5, half == 0, half == 1,
                         gu(f, c), ready, free, more)

                def turn_glu(c, more=0):
                    pe.wait_ge(dve_done.sem, dve_done.done(L, ("mul", f, c, 1), 3 * more))
                    if c > 0:
                        pe.wait_ge(dve_done.sem, dve_done.done(L, ("glulo", f, c - 1), 3 * more))
                    for j in range(2):
                        for t in range(T):
                            m = nc.tensor.transpose(ps[:, 2, j * SEQ + t * P:j * SEQ + (t + 1) * P],
                                                    glu[:, t, j * P:(j + 1) * P], ident[:, :])
                    turned.sign(m, ("glu", f, c))

                def down(c, more=0, between=None):
                    n = base + (FFN_UNITS - 1 if c == STEPS - 1 else 3 * c + 4)
                    s = n % SLOTS
                    last = c == STEPS - 1
                    pe.wait_ge(lo_split.sem, lo_split.done(L, n, 3 * more))
                    pe.wait_ge(dve_done.sem, dve_done.done(L, ("glulo", f, c), 3 * more))
                    for t in range(T):
                        if between and t == 1:
                            between()
                        for j in range(2):
                            for h in range(2):
                                at = j * D + h * W5
                                m = passes(ps[:, 4 + 2 * t + h, :], glu_hi[c % 2][:, j, t * P:(t + 1) * P],
                                           glu_lo[c % 2][:, j, t * P:(t + 1) * P],
                                           w_hi[:, s, at:at + W5], w_lo[:, s, at:at + W5], c == 0 and j == 0, last and j == 1)
                        if last and t == 0:
                            acc_done.sign(m, ("down", f))
                    unit_used.sign(m, n)

                def step(c, more=0, between=None):
                    gate_up(c, 0, more)
                    turn_glu(c - 1, more)
                    gate_up(c, 1, more)
                    down(c - 1, more, between)

                gate_up(0, 0, between=inside_first)
                gate_up(0, 1)
                step(1)
                with pe.Fori(0, STEPS - 3, TURN) as more:
                    for i in range(TURN):
                        step(2 + i, more)
                for s_, per in ((unit_used, 3), (acc_done, 1), (turned, 1)):
                    s_.skip(per * (STEPS - 3 - TURN))
                step(STEPS - 1, between=lambda: turn_glu(STEPS - 1))
                down(STEPS - 1)

            def after(L, steps, name):
                pe.wait_ge(steps.sem, steps.done(L, name))

            FREE = {}
            for n in ("fg", "q", "k", "v", "sv", "su", "ac", "ab", "g1", "g2", "g3", "g4", "g5", "g6",
                      "xk0", "xk1", "xq0", "xq1", "xv0", "xv1"):
                FREE[n] = lambda t, n=n: (act_done, (n, t))
            FREE["ah"] = lambda t: (dve_done, ("az", t))
            for n in ("c0", "c1", "b0", "b1", "a0", "a1"):
                FREE[n] = lambda t, n=n: (dve_done, (n, t))
            for n, w, h in (("wo0", "wo", 0), ("wo1", "wo", 1), ("xo0", "xo", 0), ("xo1", "xo", 1)):
                FREE[n] = lambda t, w=w, h=h: (dve_done, ("x", w, t, h))
            TILES = dict(BLOCKS)

            def run_unit(L, name, i, s_hi, s_lo, at0=0, ready=None):
                tiles = TILES[name][i]
                width = GATE if name == "fg" or name[0] == "g" else W5

                def free(t):
                    if i == 0 and name in BEFORE:
                        after(L, *FREE[BEFORE[name]](t))

                unit(L, name, FIRST[name] + i, s_hi, s_lo, at0, tiles, 2 * PAIR[name], width, i == 0,
                     i == len(TILES[name]) - 1, name, ready, free)

            def run(L, name, s_hi, s_lo):
                run_unit(L, name, 0, s_hi, s_lo)
                run_unit(L, name, 1, s_hi, s_lo)

            pe.sem_inc(unit_used.sem, unit_used.start)
            pe.wait_ge(ident_made, 2)
            with pe.Fori(0, LAYERS) as L:
                def turn_x(h):
                    for t in range(T):
                        pe.wait_ge(dve_done.sem, dve_done.done_before(L, 3 - TH1.index((t, h))))
                        pe.wait_ge(x_loaded[t], 16)
                        turn(L, x, "x", "ffn1", t, h)

                turn_x(0)
                ffn(L, 1, lambda: turn_x(1))

                def turn_mix(h):
                    for t in range(T):
                        after(L, dve_done, ("x", "f1", t, h))
                        turn(L, x, "x", "mix", t, h)

                def ready_fg(i, t):
                    if i == 0 and t == 1:
                        turn_mix(1)
                    after(L, dve_done, ("lo", "mix", t, i))

                turn_mix(0)
                for i in range(2):
                    run_unit(L, "fg", i, h_hi, h_lo, ready=lambda t, i=i: ready_fg(i, t))
                run(L, "q", h_hi, h_lo)
                after(L, dve_done, "logf")
                pe.wait_ge(consts_made, CONSTS)
                nc.tensor.matmul(ps[:, 7, 0:SEQ], log_f[:, 0, :], neg_upper[:, :], start=True, stop=False, skip_group_check=True)
                nc.tensor.matmul(ps[:, 7, P:SEQ], log_f[:, 1, :], neg_upper[:, 0:P], start=False, stop=True, skip_group_check=True)
                by_head = [log_f[:, t, 0:HEADS] for t in range(T)]
                nc.tensor.matmul(ps[:, 7, SEQ:SEQ + 8], neg_upper[:, 0:P], by_head[0], start=True, stop=True, skip_group_check=True)
                nc.tensor.matmul(ps[:, 7, SEQ + 8:SEQ + 16], neg_upper[:, P:SEQ], by_head[0], start=True, stop=False, skip_group_check=True)
                mixed.sign(nc.tensor.matmul(ps[:, 7, SEQ + 8:SEQ + 16], neg_upper[:, 0:P], by_head[1], start=False, stop=True,
                                            skip_group_check=True), "c")
                run(L, "k", h_hi, h_lo)
                after(L, act_done, ("q", 1))
                turn_pair(L, q, 4, "q")
                run(L, "v", h_hi, h_lo)
                after(L, act_done, ("k", 1))
                after(L, act_done, "negcq")
                after(L, dve_done, "neglo")
                turn_pair(L, k, 6, "k")
                run(L, "sv", h_hi, h_lo)

                def scores(L, part):
                    bank, width, first, n, tile = {0: (4, P, 0, 8, 0), 1: (6, SEQ, 0, 4, 1), 2: (4, SEQ, 4, 4, 1)}[part]
                    for i in range(n):
                        h = first + i
                        rows = slice(HD * (h % 2), HD * (h % 2) + HD)
                        o = ps[:, bank + i % 2, i // 2 * width:(i // 2 + 1) * width]
                        nc.tensor.matmul(o, qt[rows, h // 2, tile * P:(tile + 1) * P], kt[rows, h // 2, 0:width],
                                         start=True, stop=False, skip_group_check=True)
                        nc.tensor.matmul(o, head_row[:, h, :], neg_c[:, 0:width], start=False, stop=False, skip_group_check=True)
                        m = nc.tensor.matmul(o[:, width - P:width], ident_bf[:, :], mask_bf[:, :], start=False, stop=True,
                                             skip_group_check=True)
                    mixed.sign(m, f"s{part}")

                after(L, act_done, "kt")
                scores(L, 0)
                run_unit(L, "su", 0, h_hi, h_lo)
                scores(L, 1)
                run_unit(L, "su", 1, h_hi, h_lo)
                run_unit(L, "ac", 0, h_hi, h_lo)
                after(L, act_done, "e0")
                scores(L, 2)
                run_unit(L, "ac", 1, h_hi, h_lo)

                after(L, dve_done, "pn1")
                for h in range(4):
                    nc.tensor.transpose(ps[:, 6 + h // 2, (h % 2) * SEQ:(h % 2) * SEQ + P], p0[:, h, :], ident[:, :])
                    m = nc.tensor.transpose(ps[:, 6 + h // 2, (h % 2) * SEQ + P:(h % 2) * SEQ + SEQ], p1[:, h, 0:P], ident[:, :])
                turned.sign(m, "p0")
                run_unit(L, "ah", 0, h_hi, h_lo)
                after(L, dve_done, "pn2")
                for h in range(4, 8):
                    nc.tensor.transpose(ps[:, 2 + h // 2, (h % 2) * SEQ:(h % 2) * SEQ + P], p0[:, h, :], ident[:, :])
                    m = nc.tensor.transpose(ps[:, 2 + h // 2, (h % 2) * SEQ + P:(h % 2) * SEQ + SEQ], p1[:, h, 0:P], ident[:, :])
                turned.sign(m, "p1")
                run_unit(L, "ah", 1, h_hi, h_lo)
                after(L, act_done, "pt0")
                for h in range(8):
                    m = nc.tensor.transpose(ps[:, 6 + h // 4, (h % 4) * P:(h % 4 + 1) * P], p1[:, h, P:SEQ], ident[:, :])
                turned.sign(m, "p2")
                run_unit(L, "ab", 0, h_hi, h_lo)
                after(L, act_done, "pt2")
                for h in range(HEADS):
                    rows = slice(HD * (h % 2), HD * (h % 2) + HD)
                    at = (h // 2 % 2) * SEQ
                    nc.tensor.matmul(ps[rows, 4 + h // 4, at:at + SEQ], v[:, 0, h * HD:(h + 1) * HD], pt0[:, h, :],
                                     start=True, stop=False, skip_group_check=True)
                    m = nc.tensor.matmul(ps[rows, 4 + h // 4, at + P:at + SEQ], v[:, 1, h * HD:(h + 1) * HD], pt1[:, h, :],
                                         start=False, stop=True, skip_group_check=True)
                mixed.sign(m, "pv")
                run_unit(L, "ab", 1, h_hi, h_lo)
                after(L, dve_done, ("vb", 1))
                after(L, pool_done, "sgw")
                for t in range(T):
                    for g in range(GROUPS):
                        m = nc.tensor.matmul(ps[:, 6 + t, g * P:(g + 1) * P], sgw[:, g * P:(g + 1) * P], vb[:, t, g * P:(g + 1) * P],
                                             start=True, stop=True, skip_group_check=True)
                mixed.sign(m, "sg")
                run_unit(L, "g1", 0, h_hi, h_lo)
                after(L, dve_done, "yclo")
                after(L, dve_done, ("az", 1))
                turn_pair(L, az, 4, "z")
                run_unit(L, "g1", 1, h_hi, h_lo)
                after(L, dve_done, ("yb", 1))
                after(L, act_done, ("ab", 1))
                turn_pair(L, ab, 6, "ab")
                run_unit(L, "g2", 0, h_hi, h_lo)
                after(L, act_done, "zp")
                turn_pair(L, u, 4, "yb")
                run_unit(L, "g2", 1, h_hi, h_lo)
                for n in ("g3", "g4", "g5", "g6"):
                    run(L, n, h_hi, h_lo)
                after(L, dve_done, "yalo")
                for i in range(2):
                    run_unit(L, f"c{i}", 0, y_hi, y_lo, 0)
                pe.wait_ge(mem_loaded, L * 16 + 16)
                for t, h in TH2:
                    turn(L, mem, "mem", "mem", t, h)
                for i in range(2):
                    run_unit(L, f"b{i}", 0, y_hi, y_lo, 4)
                run_unit(L, "a0", 0, y_hi, y_lo, 8)
                run_unit(L, "a1", 0, y_hi, y_lo, 8)
                after(L, dve_done, ("lo", "mem", 1, 1))
                run_unit(L, "xk0", 0, y_hi, y_lo)
                after(L, pool_done, ("add", "a1", 1))
                for t, h in TH2:
                    turn(L, merged, "mg", "mg", t, h)
                run_unit(L, "xk0", 1, y_hi, y_lo)
                after(L, dve_done, ("lo", "mg", 1, 1))
                run_unit(L, "wo0", 0, h_hi, h_lo)
                run_unit(L, "wo0", 1, h_hi, h_lo)
                after(L, act_done, ("xk0", 1))
                turn_pair(L, xk, 4, "xk0")
                run_unit(L, "wo0", 2, h_hi, h_lo)
                run(L, "wo1", h_hi, h_lo)
                after(L, act_done, "xkt0")
                for t in range(T):
                    after(L, dve_done, ("x", "wo", t, 0))
                    turn(L, x, "x", "xa", t, 0)
                run_unit(L, "xk1", 0, y_hi, y_lo)
                for t in range(T):
                    after(L, dve_done, ("x", "wo", t, 1))
                    turn(L, x, "x", "xa", t, 1)
                run_unit(L, "xk1", 1, y_hi, y_lo)
                for i in range(2):
                    run_unit(L, "xq0", i, h_hi, h_lo, ready=lambda t, i=i: after(L, dve_done, ("lo", "xa", t, i)))
                after(L, act_done, ("xk1", 1))
                turn_pair(L, xk, 4, "xk1")
                run_unit(L, "xq1", 0, h_hi, h_lo)
                after(L, act_done, ("xq0", 1))
                turn_pair(L, xq[0], 6, "xq0")
                run_unit(L, "xq1", 1, h_hi, h_lo)

                def xscores(L, part):
                    for t in range(T):
                        for j in range(2):
                            for c in range(2):
                                kk = 4 * part + 2 * j + c
                                m = nc.tensor.matmul(ps[:, 4 + t, j * SEQ:(j + 1) * SEQ], xqt[:, kk, t * P:(t + 1) * P], xkt[:, kk, :],
                                                     start=c == 0, stop=c == 1, skip_group_check=True)
                    mixed.sign(m, "xs" + "ab"[part])

                after(L, act_done, "xqt0")
                xscores(L, 0)
                run_unit(L, "xv0", 0, y_hi, y_lo)
                after(L, act_done, ("xq1", 1))
                turn_pair(L, xq[1], 6, "xq1")
                run_unit(L, "xv0", 1, y_hi, y_lo)
                after(L, act_done, "xqt1")
                xscores(L, 1)

                def xturn(L, part, bank):
                    after(L, dve_done, "xpn" + "ab"[part])
                    for h in range(2):
                        for kk in range(2):
                            for t in range(T):
                                m = nc.tensor.transpose(ps[:, bank + h, kk * SEQ + t * P:kk * SEQ + (t + 1) * P],
                                                        xp[part][:, t, h * SEQ + kk * P:h * SEQ + (kk + 1) * P], ident[:, :])
                    turned.sign(m, "xp" + "ab"[part])

                run_unit(L, "xv1", 0, y_hi, y_lo)
                xturn(L, 0, 6)
                run_unit(L, "xv1", 1, y_hi, y_lo)
                xturn(L, 1, 4)

                def xvalues(L, part, bank):
                    for h in range(2):
                        for c in range(2):
                            for kk in range(2):
                                at = (2 * part + h) * SEQ + c * P
                                m = nc.tensor.matmul(ps[:, bank + h, c * SEQ:(c + 1) * SEQ], xv[:, kk, at:at + P],
                                                     xpt[:, 2 * part + h, kk, :], start=kk == 0, stop=kk == 1, skip_group_check=True)
                    mixed.sign(m, "xv" + "ab"[part])

                after(L, act_done, "xpt0")
                xvalues(L, 0, 6)
                after(L, act_done, "xpt1")
                xvalues(L, 1, 4)
                after(L, dve_done, "oalo")
                run_unit(L, "xo0", 0, h_hi, h_lo)
                after(L, dve_done, "oblo")
                run_unit(L, "xo0", 1, h_hi, h_lo)
                run_unit(L, "xo1", 0, h_hi, h_lo)
                for t in range(T):
                    after(L, dve_done, ("x", "xo", t, 0))
                    turn(L, x, "x", "ffn2", t, 0)
                run_unit(L, "xo1", 1, h_hi, h_lo)

                def turn_second_half():
                    for t in range(T):
                        after(L, dve_done, ("x", "xo", t, 1))
                        turn(L, x, "x", "ffn2", t, 1)

                ffn(L, 2, turn_second_half)


_INS = ["weights", "x", "mem", "params", "sg_norm", "sg_w", "fox_b_f", "final_norm"]


def _layout(i):
    import numpy as np

    def tiles(w, rows, cols):
        u = np.zeros((P, UNIT), w.dtype)
        for j, r in enumerate(rows):
            part = w[r * P:(r + 1) * P, cols]
            u[:, j * W5:j * W5 + part.shape[1]] = part
        return u

    units = []
    w_in_cols = {}
    names = ["ab", "ac", "ah", "su", "sv", "q", "k", "v"]
    for n, name in enumerate(names):
        w_in_cols[name] = slice(n * W5, (n + 1) * W5)
    for n, name in enumerate(["fg", "g1", "g2", "g3", "g4", "g5", "g6"]):
        w_in_cols[name] = slice(8 * W5 + n * GATE, 8 * W5 + (n + 1) * GATE)

    def ffn_units(l, f):
        g, up, dn = (np.asarray(i[f"ffn{f}_w_{n}"][l]) for n in ("gate", "up", "down"))

        def gate_up(c, half):
            u = np.empty((P, 4, 2, FC), g.dtype)
            for j in range(4):
                r = slice((4 * half + j) * P, (4 * half + j + 1) * P)
                u[:, j, 0] = g[r, c * FC:(c + 1) * FC]
                u[:, j, 1] = up[r, c * FC:(c + 1) * FC]
            return u.reshape(P, UNIT)

        def down(c):
            return dn[c * FC:(c + 1) * FC].reshape(2, P, D).transpose(1, 0, 2).reshape(P, UNIT)

        out = [gate_up(0, 0), gate_up(0, 1)]
        for c in range(1, STEPS):
            out += [gate_up(c, 0), gate_up(c, 1), down(c - 1)]
        return out + [down(STEPS - 1)]

    for l in range(LAYERS):
        units += ffn_units(l, 1)
        for name, parts in BLOCKS:
            half = slice(int(name[-1]) * W5, (int(name[-1]) + 1) * W5) if name[-1].isdigit() else None
            if name in w_in_cols:
                w, cols = np.asarray(i["w_in"][l]), w_in_cols[name]
            elif name[0] in "abc":
                w, cols = np.asarray(i["w_branch"][l]["abc".index(name[0])]), half
            elif name[:2] == "wo":
                w, cols = np.asarray(i["w_out"][l]), half
            else:
                w, cols = np.asarray(i["xa_w" + name[1]][l]), half
            units += [tiles(w, r, cols) for r in parts]
        units += ffn_units(l, 2)
    params = []
    for l in range(LAYERS):
        cols = [np.asarray(i[n][l]).reshape(KT, P).T for n in ("ffn1_norm", "mix_norm", "mem_norm", "xa_norm", "ffn2_norm")]
        cols.append(np.asarray(i["conv_w"][l]).reshape(3 * 4, P).T)
        cols.append(np.asarray(i["sg_b"][l]).T)
        params.append(np.concatenate(cols, axis=1))
    return {
        "weights": np.stack(units),
        "x": np.asarray(i["x"]).reshape(SEQ, D),
        "mem": np.asarray(i["mem"]).reshape(SEQ, D),
        "params": np.stack(params),
        "sg_norm": np.asarray(i["sg_norm"]),
        "sg_w": np.asarray(i["sg_w"]).transpose(0, 3, 1, 2).reshape(LAYERS, P, GROUPS * P),
        "fox_b_f": np.asarray(i["fox_b_f"]),
        "final_norm": np.asarray(i["final_norm"]).reshape(1, D),
    }


def kernel(**inputs):
    import numpy as _np
    import concourse.bacc as _bacc
    from concourse.bass_utils import run_bass_kernel_spmd as _run

    nc = _bacc.Bacc("TRN2", target_bir_lowering=False, num_devices=1)
    laid = _layout(inputs)
    arrays, args = {}, []
    for name in _INS:
        a = _np.ascontiguousarray(laid[name])
        arrays[f"in_{name}"] = a
        args.append(nc.dram_tensor(f"in_{name}", a.shape, mybir.dt.from_np(a.dtype), kind="ExternalInput").ap())
    out = nc.dram_tensor("out_0", (SEQ, D), F32, kind="ExternalOutput").ap()
    trunk(nc, *args, out)
    r = _run(nc, [arrays], core_ids=[0])
    return r.results[0]["out_0"].reshape(1, SEQ, D)
```
